# Optimizing a Trainium2 kernel written in Bass

```python
import math
import jax
import jax.numpy as jnp
from jax import lax
import numpy as np
import jax, jax.numpy as jnp

D_MODEL = 2048
BATCH = 1
SEQ = 256
DEPTH = 1

BLOCK = 128
N_BRANCH = 4
BRANCH_W = D_MODEL // 4
A_HEADS = 4
A_HD = BRANCH_W // (2 * A_HEADS)
B_WIDTH = BRANCH_W
B_BLOCKS = 8
B_CONV = 4
B_C = 8.0
C_HEADS = 4
C_HD = BRANCH_W // C_HEADS
D_HEADS = 8
D_KV = 2
D_GROUP = D_HEADS // D_KV
D_HD = BRANCH_W // D_HEADS
WINDOW = 128
D_FF = -(-8 * D_MODEL // (3 * 256)) * 256

IN_SIZES = (
    2 * A_HEADS * A_HD, 2 * A_HEADS * A_HD, 2 * A_HEADS * A_HD,
    B_WIDTH, B_WIDTH,
    C_HEADS * C_HD, C_HEADS * C_HD, C_HEADS * C_HD, C_HEADS,
    D_HEADS * D_HD, D_KV * D_HD, D_KV * D_HD,
    N_BRANCH * D_MODEL,
)
IN_COLS = sum(IN_SIZES)
RMS_EPS = 1e-6
NEG_INF = -1e30


def rms_norm(x, g):
    xf = x.astype(jnp.float32)
    y = xf * lax.rsqrt(jnp.mean(xf * xf, axis=-1, keepdims=True) + RMS_EPS)
    return (y * g.astype(jnp.float32)).astype(x.dtype)

def alibi_slopes(n):
    return jnp.exp2(-8.0 * jnp.arange(1, n + 1, dtype=jnp.float32) / n)

def diff_attention(q, k, v, lam, slopes):
    B, S, H, _, dh = q.shape
    nb = S // BLOCK
    scale = dh ** -0.5
    qb = q.reshape(B, nb, BLOCK, H, 2, dh).transpose(1, 0, 2, 3, 4, 5)
    kpos = jnp.arange(S)

    def one_block(args):
        qblk, i = args
        qpos = i * BLOCK + jnp.arange(BLOCK)
        dist = (qpos[:, None] - kpos[None, :]).astype(jnp.float32)
        logits = jnp.einsum('bqhmd,bshmd->bmhqs', qblk, k).astype(jnp.float32) * scale
        logits = logits - slopes[:, None, None] * dist
        logits = jnp.where(dist >= 0, logits, NEG_INF)
        p = jax.nn.softmax(logits, axis=-1)
        w = p[:, 0] - lam * p[:, 1]
        return jnp.einsum('bhqs,bshe->bqhe', w.astype(v.dtype), v)

    out = lax.map(one_block, (qb, jnp.arange(nb)))
    return out.transpose(1, 0, 2, 3, 4).reshape(B, S, H, 2 * dh)

def rg_lru_branch(xb, gb, conv_w, conv_b, wa, ba, wx, bx, lam):
    B, S, C = xb.shape
    xc = lax.conv_general_dilated(xb, conv_w[:, None, :], window_strides=(1,),
                                  padding=[(B_CONV - 1, 0)],
                                  dimension_numbers=('NWC', 'WIO', 'NWC'),
                                  feature_group_count=C) + conv_b
    xg = xc.reshape(B, S, B_BLOCKS, C // B_BLOCKS)
    r = jax.nn.sigmoid(jnp.einsum('bsnc,ncd->bsnd', xg, wa).reshape(B, S, C) + ba)
    i = jax.nn.sigmoid(jnp.einsum('bsnc,ncd->bsnd', xg, wx).reshape(B, S, C) + bx)
    log_a = -B_C * r.astype(jnp.float32) * jax.nn.softplus(-lam.astype(jnp.float32))
    a = jnp.exp(log_a)
    u = jnp.sqrt(-jnp.expm1(2.0 * log_a)) * (i * xc).astype(jnp.float32)

    def combine(left, right):
        a1, b1 = left
        a2, b2 = right
        return a1 * a2, a2 * b1 + b2

    _, h = lax.associative_scan(combine, (a, u), axis=1)
    return jax.nn.gelu(gb) * h.astype(xb.dtype)

def forgetting_attention(q, k, v, logf):
    B, S, H, dh = q.shape
    nb = S // BLOCK
    scale = dh ** -0.5
    cum = jnp.cumsum(logf, axis=1).transpose(0, 2, 1)
    qb = q.reshape(B, nb, BLOCK, H, dh).transpose(1, 0, 2, 3, 4)
    cqb = cum.reshape(B, H, nb, BLOCK).transpose(2, 0, 1, 3)
    kpos = jnp.arange(S)

    def one_block(args):
        qblk, cq, i = args
        qpos = i * BLOCK + jnp.arange(BLOCK)
        causal = qpos[:, None] >= kpos[None, :]
        logits = jnp.einsum('bqhd,bshd->bhqs', qblk, k).astype(jnp.float32) * scale
        logits = logits + cq[..., None] - cum[:, :, None, :]
        logits = jnp.where(causal, logits, NEG_INF)
        p = jax.nn.softmax(logits, axis=-1)
        return jnp.einsum('bhqs,bshd->bqhd', p.astype(v.dtype), v)

    out = lax.map(one_block, (qb, cqb, jnp.arange(nb)))
    return out.transpose(1, 0, 2, 3, 4).reshape(B, S, H * dh)

def sliding_window_sink_attention(q, k, v, sinks, slopes):
    B, S, KV, G, dh = q.shape
    nb = S // BLOCK
    scale = dh ** -0.5
    pad = ((0, 0), (BLOCK, 0), (0, 0), (0, 0))

    def band(t):
        tp = jnp.pad(t, pad)
        prev = tp[:, :S].reshape(B, nb, BLOCK, KV, dh)
        cur = tp[:, BLOCK:].reshape(B, nb, BLOCK, KV, dh)
        return jnp.concatenate([prev, cur], axis=2)

    kb, vb = band(k), band(v)
    qb = q.reshape(B, nb, BLOCK, KV, G, dh)
    qi = jnp.arange(BLOCK)
    kj = jnp.arange(2 * BLOCK) - BLOCK
    dist = (qi[:, None] - kj[None, :]).astype(jnp.float32)
    key_pos = jnp.arange(nb)[:, None] * BLOCK + kj[None, :]
    valid = ((dist >= 0) & (dist < WINDOW))[None] & (key_pos >= 0)[:, None, :]
    logits = jnp.einsum('bnqkgd,bnskd->bnkgqs', qb, kb).astype(jnp.float32) * scale
    logits = logits - slopes.reshape(KV, G)[:, :, None, None] * dist
    logits = jnp.where(valid[None, :, None, None], logits, NEG_INF)
    sink = sinks.astype(jnp.float32).reshape(KV, G)[None, None, :, :, None, None]
    m = jnp.maximum(jnp.max(logits, axis=-1, keepdims=True), sink)
    e = jnp.exp(logits - m)
    p = e / (jnp.sum(e, axis=-1, keepdims=True) + jnp.exp(sink - m))
    out = jnp.einsum('bnkgqs,bnskd->bnqkgd', p.astype(v.dtype), vb)
    return out.reshape(B, S, KV * G * dh)

def first_inputs(seed: int = 0) -> dict:
    key = jax.random.key(seed)
    ks = jax.random.split(key, 26)
    f32 = jnp.float32

    def nrm(k, shape, scale):
        return jax.random.normal(k, shape, f32) * scale

    bw = B_WIDTH // B_BLOCKS
    a8 = jax.random.uniform(ks[15], (DEPTH, B_WIDTH), f32, 0.9, 0.999)
    a0 = a8 ** (1.0 / B_C)
    return {
        'x': nrm(ks[0], (BATCH, SEQ, D_MODEL), 1.0),
        'norm_mix': 1.0 + nrm(ks[1], (DEPTH, D_MODEL), 0.02),
        'w_in': nrm(ks[2], (DEPTH, D_MODEL, IN_COLS), D_MODEL ** -0.5),
        'b_gate': nrm(ks[3], (DEPTH, N_BRANCH * D_MODEL), 0.02),
        'diff_lq1': nrm(ks[4], (DEPTH, A_HD), 0.1),
        'diff_lk1': nrm(ks[5], (DEPTH, A_HD), 0.1),
        'diff_lq2': nrm(ks[6], (DEPTH, A_HD), 0.1),
        'diff_lk2': nrm(ks[7], (DEPTH, A_HD), 0.1),
        'diff_subln': 1.0 + nrm(ks[8], (DEPTH, 2 * A_HD), 0.02),
        'lru_conv_w': nrm(ks[9], (DEPTH, B_CONV, B_WIDTH), B_CONV ** -0.5),
        'lru_conv_b': nrm(ks[10], (DEPTH, B_WIDTH), 0.02),
        'lru_wa': nrm(ks[11], (DEPTH, B_BLOCKS, bw, bw), bw ** -0.5),
        'lru_ba': nrm(ks[12], (DEPTH, B_WIDTH), 0.02),
        'lru_wx': nrm(ks[13], (DEPTH, B_BLOCKS, bw, bw), bw ** -0.5),
        'lru_bx': nrm(ks[14], (DEPTH, B_WIDTH), 0.02),
        'lru_lambda': jnp.log(a0) - jnp.log1p(-a0),
        'fox_b_f': 2.0 + nrm(ks[16], (DEPTH, C_HEADS), 0.5),
        'swa_sinks': nrm(ks[17], (DEPTH, D_HEADS), 0.5),
        'w_branch': nrm(ks[18], (DEPTH, N_BRANCH, BRANCH_W, D_MODEL), BRANCH_W ** -0.5),
        'w_out': nrm(ks[19], (DEPTH, D_MODEL, D_MODEL), D_MODEL ** -0.5),
        'norm_ffn': 1.0 + nrm(ks[20], (DEPTH, D_MODEL), 0.02),
        'w_ffn_gate': nrm(ks[21], (DEPTH, D_MODEL, D_FF), D_MODEL ** -0.5),
        'w_ffn_up': nrm(ks[22], (DEPTH, D_MODEL, D_FF), D_MODEL ** -0.5),
        'w_ffn_down': nrm(ks[23], (DEPTH, D_FF, D_MODEL), D_FF ** -0.5),
        'norm_final': 1.0 + nrm(ks[24], (D_MODEL,), 0.02),
    }

def first_block(x, norm_mix, w_in, b_gate, diff_lq1, diff_lk1, diff_lq2, diff_lk2, diff_subln,
              lru_conv_w, lru_conv_b, lru_wa, lru_ba, lru_wx, lru_bx, lru_lambda,
              fox_b_f, swa_sinks, w_branch, w_out, norm_ffn, w_ffn_gate, w_ffn_up, w_ffn_down,
              norm_final):
    B, S, _ = x.shape
    slopes_a = alibi_slopes(A_HEADS)
    slopes_d = alibi_slopes(D_HEADS)
    split_points = []
    acc = 0
    for size in IN_SIZES[:-1]:
        acc += size
        split_points.append(acc)

    h = x
    for l in range(DEPTH):
        u = rms_norm(h, norm_mix[l])
        z = u @ w_in[l]
        (aq, ak, av, bxin, bgate, cq, ck, cv, cf, dq, dk, dv, gz) = jnp.split(z, split_points, axis=-1)

        lam_init = 0.8 - 0.6 * math.exp(-0.3 * l)
        lam = (jnp.exp(jnp.sum(diff_lq1[l].astype(jnp.float32) * diff_lk1[l].astype(jnp.float32)))
               - jnp.exp(jnp.sum(diff_lq2[l].astype(jnp.float32) * diff_lk2[l].astype(jnp.float32)))
               + lam_init)
        ya = diff_attention(aq.reshape(B, S, A_HEADS, 2, A_HD), ak.reshape(B, S, A_HEADS, 2, A_HD),
                            av.reshape(B, S, A_HEADS, 2 * A_HD), lam, slopes_a)
        ya = (rms_norm(ya, diff_subln[l]) * (1.0 - lam_init)).reshape(B, S, BRANCH_W)

        yb = rg_lru_branch(bxin, bgate, lru_conv_w[l], lru_conv_b[l], lru_wa[l], lru_ba[l],
                           lru_wx[l], lru_bx[l], lru_lambda[l])

        logf = jax.nn.log_sigmoid((cf + fox_b_f[l]).astype(jnp.float32))
        yc = forgetting_attention(cq.reshape(B, S, C_HEADS, C_HD), ck.reshape(B, S, C_HEADS, C_HD),
                                  cv.reshape(B, S, C_HEADS, C_HD), logf)

        yd = sliding_window_sink_attention(dq.reshape(B, S, D_KV, D_GROUP, D_HD),
                                           dk.reshape(B, S, D_KV, D_HD), dv.reshape(B, S, D_KV, D_HD),
                                           swa_sinks[l], slopes_d)

        gates = jax.nn.sigmoid(gz + b_gate[l]).reshape(B, S, N_BRANCH, D_MODEL)
        branches = (ya, yb, yc, yd)
        mixed = gates[:, :, 0] * (branches[0] @ w_branch[l, 0])
        for n in range(1, N_BRANCH):
            mixed = mixed + gates[:, :, n] * (branches[n] @ w_branch[l, n])
        h = h + mixed @ w_out[l]

        v = rms_norm(h, norm_ffn[l])
        h = h + (jax.nn.silu(v @ w_ffn_gate[l]) * (v @ w_ffn_up[l])) @ w_ffn_down[l]

    return rms_norm(h, norm_final)


HEAD_DIM = 128
N_MEM = 256
GRID_W = 64
DIL_PAIRS = ((128, 1), (512, 4), (2048, 16))
A_HEADS_PER_GROUP = 2
A_HEADS_2 = A_HEADS_PER_GROUP * len(DIL_PAIRS)
A_BLOCK = 64
B_Q_HEADS = 6
B_KV_HEADS = 2
B_QBLOCK = 128
ROPE_THETA = 10000.0
N_BRANCH_2 = 3
REL_BUCKETS = 32
REL_MAX_DIST = 1024
D_FF_2 = -(-8 * D_MODEL // (3 * 256)) * 256
EPS = 1e-6
NEG = -1e30

A_W = A_HEADS_2 * HEAD_DIM
A_OUT_W = A_HEADS_PER_GROUP * HEAD_DIM
B_QW = B_Q_HEADS * HEAD_DIM
B_KVW = B_KV_HEADS * HEAD_DIM
C_W = C_HEADS * HEAD_DIM
IN_SPLITS = (A_W, A_W, A_W, B_QW, B_KVW, B_KVW, C_W, N_BRANCH_2 * D_MODEL)
IN_W = sum(IN_SPLITS)


def rms_norm_2(x, g):
    xf = x.astype(jnp.float32)
    y = xf * lax.rsqrt(jnp.mean(xf * xf, axis=-1, keepdims=True) + EPS)
    return (y * g.astype(jnp.float32)).astype(x.dtype)

def split_heads(t, h):
    return t.reshape(t.shape[0], t.shape[1], h, HEAD_DIM)

def t5_bucket(rel):
    nb = REL_BUCKETS // 2
    ret = jnp.where(rel > 0, nb, 0)
    n = jnp.abs(rel)
    max_exact = nb // 2
    large = max_exact + (jnp.log(jnp.maximum(n, 1).astype(jnp.float32) / max_exact)
                         / math.log(REL_MAX_DIST / max_exact) * (nb - max_exact)).astype(jnp.int32)
    large = jnp.minimum(large, nb - 1)
    return ret + jnp.where(n < max_exact, n, large)

def dilated_group(q, k, v, bias_tab, window, dil):
    b, s, h, dh = q.shape
    L = s // dil
    radius = window // (2 * dil)
    n = b * dil

    def to_res(t):
        return t.reshape(b, L, dil, h, dh).transpose(0, 2, 1, 3, 4).reshape(n, L, h, dh)

    qr, kr, vr = to_res(q), to_res(k), to_res(v)
    nb = -(-L // A_BLOCK)
    lp = nb * A_BLOCK
    side = -(-radius // A_BLOCK)
    pad = side * A_BLOCK
    wk = (2 * side + 1) * A_BLOCK
    qb = jnp.pad(qr, ((0, 0), (0, lp - L), (0, 0), (0, 0))).reshape(n, nb, A_BLOCK, h, dh)

    def band(t):
        tp = jnp.pad(t, ((0, 0), (pad, lp - L + pad), (0, 0), (0, 0))).reshape(n, nb + 2 * side, A_BLOCK, h, dh)
        return jnp.concatenate([tp[:, i:i + nb] for i in range(2 * side + 1)], axis=2)

    kb, vb = band(kr), band(vr)
    rel = (jnp.arange(wk) - pad)[None, :] - jnp.arange(A_BLOCK)[:, None]
    bias = bias_tab[t5_bucket(rel * dil)].transpose(2, 0, 1).astype(jnp.float32)
    k_pos = jnp.arange(nb)[:, None] * A_BLOCK - pad + jnp.arange(wk)[None, :]
    valid = (jnp.abs(rel) <= radius)[None] & ((k_pos >= 0) & (k_pos < L))[:, None, :]
    sc = jnp.einsum('nbqhd,nbkhd->nbhqk', qb, kb, preferred_element_type=jnp.float32) / math.sqrt(dh)
    sc = jnp.where(valid[None, :, None], sc + bias[None, None], NEG)
    m = jnp.max(sc, axis=-1, keepdims=True)
    p = jnp.exp(sc - m)
    l = jnp.sum(p, axis=-1, keepdims=True)
    o = jnp.einsum('nbhqk,nbkhd->nbqhd', p, vb.astype(jnp.float32))
    o = o / l[..., 0].transpose(0, 1, 3, 2)[..., None]
    lse = (m + jnp.log(l))[..., 0].transpose(0, 1, 3, 2)
    o = o.reshape(n, lp, h, dh)[:, :L]
    lse = lse.reshape(n, lp, h)[:, :L]
    o = o.reshape(b, dil, L, h, dh).transpose(0, 2, 1, 3, 4).reshape(b, s, h, dh)
    lse = lse.reshape(b, dil, L, h).transpose(0, 2, 1, 3).reshape(b, s, h)
    return o, lse

def axial_rope_tables(s):
    rows = s // GRID_W
    r = jnp.repeat(jnp.arange(rows), GRID_W).astype(jnp.float32)
    c = jnp.tile(jnp.arange(GRID_W), rows).astype(jnp.float32)
    nf = HEAD_DIM // 4
    inv = ROPE_THETA ** (-jnp.arange(nf, dtype=jnp.float32) / nf)
    ang = jnp.concatenate([r[:, None] * inv, c[:, None] * inv], axis=-1)
    return jnp.cos(ang), jnp.sin(ang)

def apply_rope(x, cos, sin):
    b, s, h, dh = x.shape
    xf = x.astype(jnp.float32).reshape(b, s, h, dh // 2, 2)
    x0, x1 = xf[..., 0], xf[..., 1]
    c, sn = cos[None, :, None, :], sin[None, :, None, :]
    out = jnp.stack([x0 * c - x1 * sn, x0 * sn + x1 * c], axis=-1)
    return out.reshape(b, s, h, dh).astype(x.dtype)

def gqa_blocks(q, k, v):
    b, s, hq, dh = q.shape
    g = hq // B_KV_HEADS
    nblk = s // B_QBLOCK
    qb = q.reshape(b, nblk, B_QBLOCK, B_KV_HEADS, g, dh).transpose(1, 0, 2, 3, 4, 5)

    def one_block(qq):
        sc = jnp.einsum('bqkgd,bskd->bkgqs', qq, k, preferred_element_type=jnp.float32) / math.sqrt(dh)
        p = jax.nn.softmax(sc, axis=-1)
        return jnp.einsum('bkgqs,bskd->bqkgd', p, v.astype(jnp.float32)).astype(q.dtype)

    o = lax.map(one_block, qb)
    return o.transpose(1, 0, 2, 3, 4, 5).reshape(b, s, hq * dh)

def second_inputs(seed: int = 0) -> dict:
    key = jax.random.key(seed)
    ks = jax.random.split(key, 24)
    f32 = jnp.float32

    def w(k, shape, fan_in):
        return jax.random.normal(k, shape, f32) * (fan_in ** -0.5)

    def gain(k, shape):
        return 1.0 + 0.05 * jax.random.normal(k, shape, f32)

    Dp = DEPTH
    return {
        "x": jax.random.normal(ks[0], (BATCH, SEQ, D_MODEL), f32),
        "mem": jax.random.normal(ks[1], (BATCH, N_MEM, D_MODEL), f32),
        "rel_bias": 0.5 * jax.random.normal(ks[2], (REL_BUCKETS, A_HEADS_2), f32),
        "g_mix": gain(ks[3], (Dp, D_MODEL)),
        "w_in": w(ks[4], (Dp, D_MODEL, IN_W), D_MODEL),
        "g_qa": gain(ks[5], (Dp, HEAD_DIM)),
        "g_ka": gain(ks[6], (Dp, HEAD_DIM)),
        "g_qb": gain(ks[7], (Dp, HEAD_DIM)),
        "g_kb": gain(ks[8], (Dp, HEAD_DIM)),
        "g_mem": gain(ks[9], (Dp, D_MODEL)),
        "w_mem_kv": w(ks[10], (Dp, D_MODEL, 2 * C_W), D_MODEL),
        "g_qc": gain(ks[11], (Dp, HEAD_DIM)),
        "g_kc": gain(ks[12], (Dp, HEAD_DIM)),
        "w_br_a": w(ks[13], (Dp, A_OUT_W, D_MODEL), A_OUT_W),
        "w_br_b": w(ks[14], (Dp, B_QW, D_MODEL), B_QW),
        "w_br_c": w(ks[15], (Dp, C_W, D_MODEL), C_W),
        "w_o": w(ks[16], (Dp, D_MODEL, D_MODEL), D_MODEL),
        "g_ffn": gain(ks[17], (Dp, D_MODEL)),
        "w_ffn_in": w(ks[18], (Dp, D_MODEL, 2 * D_FF_2), D_MODEL),
        "w_ffn_out": w(ks[19], (Dp, D_FF_2, D_MODEL), D_FF_2),
    }

def second_block(x, mem, rel_bias, g_mix, w_in, g_qa, g_ka, g_qb, g_kb, g_mem, w_mem_kv,
              g_qc, g_kc, w_br_a, w_br_b, w_br_c, w_o, g_ffn, w_ffn_in, w_ffn_out):
    b, s, _ = x.shape
    cos, sin = axial_rope_tables(s)
    offs = np.cumsum((0,) + IN_SPLITS)
    for layer in range(DEPTH):
        h = rms_norm_2(x, g_mix[layer])
        proj = h @ w_in[layer]
        qa, ka, va, qb, kb, vb, qc, gt = [proj[..., offs[i]:offs[i + 1]] for i in range(len(IN_SPLITS))]

        qa = rms_norm_2(split_heads(qa, A_HEADS_2), g_qa[layer])
        ka = rms_norm_2(split_heads(ka, A_HEADS_2), g_ka[layer])
        va = split_heads(va, A_HEADS_2)
        outs, lses = [], []
        for gi, (win, dil) in enumerate(DIL_PAIRS):
            sl = slice(gi * A_HEADS_PER_GROUP, (gi + 1) * A_HEADS_PER_GROUP)
            o, lse = dilated_group(qa[:, :, sl], ka[:, :, sl], va[:, :, sl], rel_bias[:, sl], win, dil)
            outs.append(o)
            lses.append(lse)
        wgt = jax.nn.softmax(jnp.stack(lses), axis=0)
        oa = jnp.sum(wgt[..., None] * jnp.stack(outs), axis=0).reshape(b, s, A_OUT_W).astype(x.dtype)

        qb = apply_rope(rms_norm_2(split_heads(qb, B_Q_HEADS), g_qb[layer]), cos, sin)
        kb = apply_rope(rms_norm_2(split_heads(kb, B_KV_HEADS), g_kb[layer]), cos, sin)
        ob = gqa_blocks(qb, kb, split_heads(vb, B_KV_HEADS))

        mkv = rms_norm_2(mem, g_mem[layer]) @ w_mem_kv[layer]
        kc = rms_norm_2(split_heads(mkv[..., :C_W], C_HEADS), g_kc[layer])
        vc = split_heads(mkv[..., C_W:], C_HEADS)
        qc = rms_norm_2(split_heads(qc, C_HEADS), g_qc[layer])
        sc = jnp.einsum('bqhd,bmhd->bhqm', qc, kc, preferred_element_type=jnp.float32) / math.sqrt(HEAD_DIM)
        pc = jax.nn.softmax(sc, axis=-1)
        oc = jnp.einsum('bhqm,bmhd->bqhd', pc, vc.astype(jnp.float32)).reshape(b, s, C_W).astype(x.dtype)

        gates = jax.nn.sigmoid(gt.astype(jnp.float32)).reshape(b, s, N_BRANCH_2, D_MODEL)
        merged = (gates[:, :, 0] * (oa @ w_br_a[layer]).astype(jnp.float32)
                  + gates[:, :, 1] * (ob @ w_br_b[layer]).astype(jnp.float32)
                  + gates[:, :, 2] * (oc @ w_br_c[layer]).astype(jnp.float32)).astype(x.dtype)
        x = x + merged @ w_o[layer]

        hf = rms_norm_2(x, g_ffn[layer]) @ w_ffn_in[layer]
        x = x + (jax.nn.silu(hf[..., :D_FF_2]) * hf[..., D_FF_2:]) @ w_ffn_out[layer]
    return x


def setup_inputs(seed=0):
    out = dict(first_inputs(seed))
    for name, value in second_inputs(seed + 1).items():
        if name != "x":
            out[name + "_2"] = value
    return out


def reference(
    x, norm_mix, w_in, b_gate, diff_lq1, diff_lk1, diff_lq2, diff_lk2, diff_subln, lru_conv_w,
    lru_conv_b, lru_wa, lru_ba, lru_wx, lru_bx, lru_lambda, fox_b_f, swa_sinks, w_branch, w_out,
    norm_ffn, w_ffn_gate, w_ffn_up, w_ffn_down, norm_final, mem_2, rel_bias_2, g_mix_2, w_in_2,
    g_qa_2, g_ka_2, g_qb_2, g_kb_2, g_mem_2, w_mem_kv_2, g_qc_2, g_kc_2, w_br_a_2, w_br_b_2,
    w_br_c_2, w_o_2, g_ffn_2, w_ffn_in_2, w_ffn_out_2,
):
    x = first_block(
        x, norm_mix, w_in, b_gate, diff_lq1, diff_lk1, diff_lq2, diff_lk2, diff_subln,
        lru_conv_w, lru_conv_b, lru_wa, lru_ba, lru_wx, lru_bx, lru_lambda, fox_b_f, swa_sinks,
        w_branch, w_out, norm_ffn, w_ffn_gate, w_ffn_up, w_ffn_down, norm_final,
    )
    return second_block(
        x, mem_2, rel_bias_2, g_mix_2, w_in_2, g_qa_2, g_ka_2, g_qb_2, g_kb_2, g_mem_2,
        w_mem_kv_2, g_qc_2, g_kc_2, w_br_a_2, w_br_b_2, w_br_c_2, w_o_2, g_ffn_2, w_ffn_in_2,
        w_ffn_out_2,
    )


_drawn_inputs = setup_inputs


def setup_inputs(seed=0):
    import zlib

    import numpy as np

    out = dict(_drawn_inputs(seed))
    spreads = {}
    factors = {'b_gate': 8.0,
     'diff_lk1': 3.684,
     'diff_lq2': 3.863,
     'diff_subln': 5.655,
     'lru_ba': 8.0,
     'lru_bx': 8.0,
     'swa_sinks': 8.0,
     'norm_ffn': 3.802,
     'g_mix_2': 5.373,
     'g_qa_2': 8.0,
     'g_ka_2': 8.0,
     'g_qb_2': 8.0,
     'g_kb_2': 8.0,
     'g_mem_2': 8.0,
     'g_qc_2': 8.0,
     'g_kc_2': 8.0,
     'g_ffn_2': 8.0}
    for name, (base, spread) in spreads.items():
        noise = np.random.default_rng([zlib.crc32(name.encode()), seed]).standard_normal(out[name].shape)
        drawn = base * np.exp(spread * noise) if base else spread * noise
        out[name] = jnp.asarray(drawn.astype(out[name].dtype))
    for name, factor in factors.items():
        out[name] = (out[name] * factor).astype(out[name].dtype)
    return out
```

```python
import math
from contextlib import ExitStack

import numpy as np

import concourse.bass as bass
from concourse import mybir

F32 = mybir.dt.float32
F32R = mybir.dt.float32r
BF16 = mybir.dt.bfloat16
ALU = mybir.AluOpType
ACT = mybir.ActivationFunctionType
AX = mybir.AxisListType.X

P = 128
SEQ = 256
D = 2048
KT = D // P
BW = 512
NB = D // BW
D_FF = 5632
FF_PARTS = (6, 5)
CHUNK_KT = 4
HALF_KT = 2
RAW_SLOTS, PART_SLOTS = 3, 4
AHEAD = 3
EPS = 1e-6
LAM_INIT = 0.8 - 0.6 * math.exp(0.0)
MASKED = -1e30
KB = 1024


class Line:

    def __init__(self, sem):
        self.sem, self.count, self.queue, self.seen = sem, 0, [], {}

    def wait(self, *tickets):
        for sem, value in tickets:
            if self.seen.get(sem.name, 0) < value:
                self.seen[sem.name] = value
                self.queue.append(lambda e, s=sem, v=value: e.wait_ge(s, v))

    def run(self, instruction):
        self.queue.append(instruction)

    def do(self, instruction):
        self.count += 1
        self.queue.append(lambda e: instruction(e).then_inc(self.sem, 1))
        return (self.sem, self.count)

    def emit(self, engine):
        for instruction in self.queue:
            instruction(engine)


class Slot:

    def __init__(self, view):
        self.view, self._users, self.held = view, [], False

    @property
    def users(self):
        return self._users

    @users.setter
    def users(self, tickets):
        self._users, self.held = tickets, False


def weight_plan():
    plan = [("w_in", b, 0, KT, BW) for b in range(5)]
    plan += [("w_in_misc", 0, 0, KT, 384)]
    plan += [("w_in", b, 0, KT, BW) for b in range(5, 9)]
    for n in range(4):
        for c in range(NB):
            plan += [("w_gates", n * NB + c, 0, KT, BW), (f"w_branch{n}", c, 0, 4, BW)]
    plan += [("w_out", b, 0, KT, BW) for b in range(NB)]

    def ffn(gate, up, down):
        out, block = [], 0
        for part in FF_PARTS:
            for b in range(block, block + part):
                out += [(gate, b, 0, KT, BW), (up, b, 0, KT, BW)]
            out += [(down, b, 4 * block, 4 * part, BW) for b in range(NB)]
            block += part
        return out

    plan += ffn("w_ffn_gate", "w_ffn_up", "w_ffn_down")
    plan += [("w_mem", b, 0, KT, BW) for b in range(2)]
    plan += [("w_in2", b, 0, KT, BW) for b in range(8)]
    for n, tiles in enumerate((4, 6, 2)):
        for c in range(NB):
            plan += [("w_gates2", n * NB + c, 0, KT, BW), (f"w_branch2{n}", c, 0, tiles, BW)]
    plan += [("w_out2", b, 0, KT, BW) for b in range(NB)]
    plan += ffn("w_ffn_gate2", "w_ffn_up2", "w_ffn_down2")
    return plan


def build(nc, dram, out):
    ctx = ExitStack()
    with ctx:
        sem_of = {n: ctx.enter_context(nc.semaphore(f"done_{n}")) for n in ("pe", "act", "dve", "pool")}
        pe, act, dve, pool = (Line(sem_of[n]) for n in ("pe", "act", "dve", "pool"))
        sp = Line(None)
        raw_landed = [ctx.enter_context(nc.semaphore(f"raw_landed{i}")) for i in range(RAW_SLOTS)]

        def load(line, to, of, sem_name=None, count=[0]):
            count[0] += 1
            sem = ctx.enter_context(nc.semaphore(sem_name or f"load{count[0]}"))
            line.run(lambda e: e.dma_start(to, of).then_inc(sem, 16))
            return (sem, 16)

        class Port:

            def __init__(self, line, name):
                self.line, self.n = line, 0
                self.sem = ctx.enter_context(nc.semaphore(name))

            def move(self, to, of):
                if self.n:
                    self.line.wait((self.sem, 16 * self.n))
                self.n += 1
                self.line.run(lambda e: e.dma_start(to, of).then_inc(self.sem, 16))
                return (self.sem, 16 * self.n)

        at = [(nc.sbuf_base + 31) // 32 * 32]

        def region(size):
            at[0] += size
            return at[0] - size

        def place(name, shape, dtype, offset):
            return nc.alloc_sbuf_tensor_at(name, [P, *shape], dtype, offset=offset)

        X_AT, RAW_AT = region(16 * KB), region(RAW_SLOTS * 8 * KB)
        HI_AT, LO_AT = region(PART_SLOTS * 4 * KB), region(PART_SLOTS * 4 * KB)
        U_AT, R_AT, Q_AT = region(32 * KB), region(48 * KB), region(48 * KB)

        resid = place("resid", [2, D], F32, X_AT)
        raw = place("raw", [RAW_SLOTS, CHUNK_KT * BW], F32, RAW_AT)
        w_hi = place("w_hi", [PART_SLOTS, HALF_KT * BW], F32R, HI_AT)
        w_lo = place("w_lo", [PART_SLOTS, HALF_KT * BW], F32R, LO_AT)

        class Split:

            def __init__(self, name, tiles, offset):
                self.hi = place(f"{name}_hi", [tiles, SEQ], F32R, offset)
                self.lo = place(f"{name}_lo", [tiles, SEQ], F32R, offset + tiles * KB)
                self.ready = {}

            def wrote(self, tiles, tickets, parts=1):
                for k in tiles:
                    self.ready.setdefault(k, []).append(tickets)
                    self.parts = parts

            def tickets(self, k):
                while len(self.ready.get(k, ())) < self.parts_of(k):
                    assert background, "a left operand that nobody writes"
                    step_background()
                return [t for group in self.ready[k] for t in group]

            def parts_of(self, k):
                return self.parts if k in self.ready else 1

        def small(name, shape, dtype=F32):
            size = int(np.prod(shape)) * (4 if dtype != BF16 else 2)
            return place(name, shape, dtype, region((size + 31) // 32 * 32))

        ident = small("ident", [P])
        diag_mask = small("diag_mask", [P])
        ones = small("ones", [SEQ])
        junk = small("junk", [BW], BF16)
        gains = small("gains", [6, KT])
        lru_cols = small("lru_cols", [8, 4])
        stats = small("stats", [192])
        tab1_at = region(3 * KB)
        dist_a = place("dist_a", [384], F32, tab1_at)
        dist_d = place("dist_d", [384], F32, tab1_at + 1536)
        rope = place("rope", [2, 2, 64], F32, tab1_at)
        head_gain_rows = place("head_gain_rows", [2, P], F32, tab1_at + KB)
        subln_col = small("subln_col", [1])
        head_gain_cols = small("head_gain_cols", [4])
        fox_bias = small("fox_bias", [1])
        onehot4 = small("onehot4", [4])
        sink_rows = small("sink_rows", [8])
        table = small("table", [6])
        minus_half = small("minus_half", [16])
        assert at[0] <= nc.sbuf_usable_end, (at[0], nc.sbuf_usable_end)

        acc = [Slot(ctx.enter_context(nc.psum_tensor(f"acc{i}", [P, 2, BW], F32))) for i in range(3)]
        misc = [Slot(ctx.enter_context(nc.psum_tensor(f"misc{i}", [P, BW], F32))) for i in range(2)]
        turn = {"acc": 0, "misc": 0}

        def take(kind, slots):
            while slots[turn[kind] % len(slots)].held:
                turn[kind] += 1
            slot = slots[turn[kind] % len(slots)]
            turn[kind] += 1
            pe.wait(*slot.users)
            slot.held = True
            return slot

        def matmul(o, w, x, start=True, stop=True):
            pe.run(lambda e: e.matmul(o, w, x, start=start, stop=stop, skip_group_check=True))

        def matmul_done(o, w, x, start=True, stop=True):
            return pe.do(lambda e: e.matmul(o, w, x, start=start, stop=stop, skip_group_check=True))

        def turn_tiles(o, tiles):
            for i, tile in enumerate(tiles):
                go = pe.do if i == len(tiles) - 1 else pe.run
                ticket = go(lambda e, i=i, tile=tile: e.transpose(o[:, i * P:(i + 1) * P], tile, ident[:, :]))
            return ticket

        def tt(line, o, a, b, op):
            return line.do(lambda e: e.tensor_tensor(o, a, b, op))

        def ts(line, o, a, s1, op0, s2=None, op1=None):
            if op1 is None:
                return line.do(lambda e: e.tensor_scalar(o, a, s1, None, op0))
            return line.do(lambda e: e.tensor_scalar(o, a, s1, s2, op0, op1))

        def stt(o, a, s, b, op0, op1):
            return dve.do(lambda e: e.scalar_tensor_tensor(o, a, s, b, op0, op1))

        def activate(o, a, func, **kw):
            return act.do(lambda e: e.activation(o, a, func, **kw))

        def scaled(o, a, scale):
            return activate(o, a, ACT.Copy, scale=scale)

        def split_store(pieces, ready):
            act.wait(*ready)
            for o_hi, _, a, scale in pieces:
                hi = activate(o_hi, a, ACT.Copy, **({} if scale is None else {"scale": scale}))
            dve.wait(*ready, hi)
            for o_hi, o_lo, a, scale in pieces:
                if scale is None:
                    lo = tt(dve, o_lo, a, o_hi.bitcast(F32), ALU.subtract)
                else:
                    lo = stt(o_lo, a, scale, o_hi.bitcast(F32), ALU.mult, ALU.subtract)
            return [hi, lo]

        used_stats = [0]

        def columns(n):
            used_stats[0] += n
            assert used_stats[0] <= 192
            return stats[:, used_stats[0] - n:used_stats[0]]

        junk_written = []

        def square_sum(a, o, ready=()):
            act.wait(*ready, *junk_written)
            junk_written[:] = [activate(junk[:, 0:a.shape[1]], a, ACT.Square, accum_out=o)]
            return junk_written[0]

        def inverse_root(o, squares, n, ready):
            pool.wait(*ready)
            t = ts(pool, o, squares, 1.0 / n, ALU.mult, EPS, ALU.add)
            pool.wait(t)
            return tt(pool, o, o, minus_half[:, 0:o.shape[1]], ALU.pow)

        const_ready = [load(pool, t[:, :] if len(t.shape) == 2 else t[:, :, :], dram[n], f"ld_{n}")
                       for t, n in ((ident, "c_ident"), (gains, "gains"))]
        ident_ready, gains_ready = const_ready
        fill_ones = pool.do(lambda e: e.memset(ones[:, :], 1.0))
        fill_half = pool.do(lambda e: e.memset(minus_half[:, :], -0.5))
        pool.wait(fill_half)
        one_row = pool.do(lambda e: e.memset(table[32:33, :], 1.0))
        pool.wait(one_row)

        plan = weight_plan()
        halves = []
        chunks = []
        for name, b, k0, kn, cols in plan:
            for k in range(k0, k0 + kn, CHUNK_KT):
                n = min(CHUNK_KT, k0 + kn - k)
                halves += [(len(chunks), o, HALF_KT, cols) for o in range(0, n, HALF_KT)]
                chunks.append((name, b, k, n, cols))
        stream = {"loaded": 0, "split": 0, "half": 0, "block": 0}
        split_done = {}
        half_read = {}
        last_split = {}
        raw_loads = [0] * RAW_SLOTS
        raw_ticket = {}

        def load_next_chunk():
            c = stream["loaded"]
            if c >= len(chunks):
                return
            name, b, k, n, cols = chunks[c]
            slot = c % RAW_SLOTS
            if c >= RAW_SLOTS:
                sp.wait(*last_split[c - RAW_SLOTS])
            raw_loads[slot] += 1
            raw_ticket[c] = (raw_landed[slot], 16 * raw_loads[slot])
            to, of = raw[:, slot, 0:n * cols], dram[name][b, :, k * cols:(k + n) * cols]
            sp.run(lambda e: e.dma_start(to, of).then_inc(raw_landed[slot], 16))
            stream["loaded"] += 1

        def split_next_half():
            h = stream["split"]
            c, o, n, cols = halves[h]
            slot = h % PART_SLOTS
            a = raw[:, c % RAW_SLOTS, o * cols:(o + n) * cols]
            hi, lo = w_hi[:, slot, 0:n * cols], w_lo[:, slot, 0:n * cols]
            act.wait(raw_ticket[c])
            if h >= PART_SLOTS:
                act.wait(half_read[h - PART_SLOTS])
            t_hi = activate(hi, a, ACT.Copy)
            dve.wait(raw_ticket[c], t_hi)
            t_lo = tt(dve, lo, a, hi.bitcast(F32), ALU.subtract)
            split_done[h] = [t_hi, t_lo]
            if h + 1 == len(halves) or halves[h + 1][0] != c:
                last_split[c] = [t_hi, t_lo]
                load_next_chunk()
            stream["split"] += 1

        def split_ahead(h):
            while stream["split"] < min(h + AHEAD + 1, len(halves)):
                split_next_half()

        background = []

        def step_background():
            if background:
                try:
                    next(background[0])
                except StopIteration:
                    background.pop(0)

        def finish(task):
            while task in background:
                step_background()

        def stream_block(name, b, left, feature_major=0):
            want, kb, k0, kn, cols = plan[stream["block"]]
            assert (want, kb) == (name, b), (want, kb, name, b)
            stream["block"] += 1
            slot = take("acc", acc)
            v = slot.view
            for j in range(kn // HALF_KT):
                h = stream["half"]
                split_ahead(h)
                pe.wait(*split_done[h])
                hi, lo = w_hi[:, h % PART_SLOTS, :], w_lo[:, h % PART_SLOTS, :]
                for i in range(HALF_KT):
                    kt = HALF_KT * j + i
                    first, last = kt == 0, kt == kn - 1
                    pe.wait(*left.tickets(kt))
                    whi = hi[:, i * cols:(i + 1) * cols]
                    wlo = lo[:, i * cols:(i + 1) * cols]
                    lhi, llo = left.hi[:, kt, :], left.lo[:, kt, :]
                    work = []
                    for f in range(feature_major):
                        o = v[:, f // 2, (f % 2) * SEQ:(f % 2 + 1) * SEQ]
                        fs = slice(f * P, (f + 1) * P)
                        work += [(o, whi[:, fs], lhi, f % 2 == 0), (o, whi[:, fs], llo, False),
                                 (o, wlo[:, fs], lhi, False)]
                    done = feature_major * P
                    if done < cols:
                        for t in range(2):
                            ts_ = slice(t * P, (t + 1) * P)
                            o = v[:, t, 0:cols] if not done else v[:, 1, t * P:(t + 1) * P]
                            clears = not done or t == 0
                            work += [(o, lhi[:, ts_], whi[:, done:cols], clears),
                                     (o, lhi[:, ts_], wlo[:, done:cols], False),
                                     (o, llo[:, ts_], whi[:, done:cols], False)]
                    for n, (o, w, x, clears) in enumerate(work):
                        if i == HALF_KT - 1 and n == len(work) - 1:
                            half_read[h] = matmul_done(o, w, x, first and clears, last)
                        else:
                            matmul(o, w, x, first and clears, last)
                stream["half"] += 1
                step_background()
            return slot, half_read[stream["half"] - 1]

        def put_tile_block(left, src, j, t, gain, ready):
            bank = take("misc", misc)
            pe.wait(*ready, ident_ready)
            done = turn_tiles(bank.view, [src[:, i * P:(i + 1) * P] for i in range(4)])
            o = slice(t * P, (t + 1) * P)
            if gain is None:
                pieces = [(left.hi[:, 4 * j:4 * j + 4, o], left.lo[:, 4 * j:4 * j + 4, o],
                           bank.view[:, :].rearrange("p (a b) -> p a b", a=4), None)]
            else:
                pieces = [(left.hi[:, k, o], left.lo[:, k, o], bank.view[:, (k - 4 * j) * P:(k - 4 * j + 1) * P],
                           gain[:, k:k + 1]) for k in range(4 * j, 4 * j + 4)]
                act.wait(gains_ready)
                dve.wait(gains_ready)
            bank.users = split_store(pieces, [done])
            left.wrote(range(4 * j, 4 * j + 4), bank.users, parts=2)

        lhs = Split("u", KT, U_AT)
        x_ready = []
        for t in range(2):
            x_ready.append(load(sp, resid[:, t, :], dram["x"][t], f"ld_x{t}"))
        for _ in range(RAW_SLOTS):
            load_next_chunk()
        ld = {}
        for n, v in (("c_diag_mask", diag_mask[:, :]), ("c_dist_a", dist_a[:, :]), ("c_dist_d", dist_d[:, :]),
                     ("lru_cols", lru_cols[:, :, :]), ("subln_col", subln_col[:, :]),
                     ("head_gain_cols", head_gain_cols[:, :]), ("fox_bias", fox_bias[0:4, :]),
                     ("c_onehot4", onehot4[0:4, :]), ("table", table[0:32, :])):
            ld[n] = load(pool, v, dram[n], f"ld_{n}")
        ld["sinks"] = load(pool, sink_rows[:, :], dram["sinks"].partition_broadcast(P), "ld_sinks")

        scaled_x = place("scaled_x", [2, D], F32, Q_AT)
        squares = columns(2)
        r_mix = columns(2)
        for t in range(2):
            act.wait(x_ready[t])
            big_junk = place(f"big_junk{t}", [D], F32, R_AT + t * 8 * KB)
            sq = activate(big_junk[:, :], resid[:, t, :], ACT.Square, accum_out=squares[:, t:t + 1])
            root = inverse_root(r_mix[:, t:t + 1], squares[:, t:t + 1], D, [sq])
            for j in range(NB):
                dve.wait(root, x_ready[t])
                cs = slice(j * BW, (j + 1) * BW)
                m = ts(dve, scaled_x[:, t, cs], resid[:, t, cs], r_mix[:, t:t + 1], ALU.mult)
                put_tile_block(lhs, scaled_x[:, t, cs], j, t, gains[:, 0, :], [m])

        def spot(name, kb, shape, base=R_AT, dtype=F32):
            return place(name, shape, dtype, base + int(kb * KB))

        aqT, akT, av = spot("aqT", 0, [4, SEQ]), spot("akT", 4, [4, SEQ]), spot("av", 8, [2, BW])
        dqT, cqT, ckT = spot("dqT", 12, [4, SEQ]), spot("cqT", 16, [4, SEQ]), spot("ckT", 20, [4, SEQ])
        cv, dkT, cfT = spot("cv", 24, [2, BW]), spot("dkT", 28, [SEQ]), spot("cfT", 29, [SEQ])
        dv = spot("dv", 30, [2, P])
        lxT, lgT = spot("lxT", 32, [4, SEQ]), spot("lgT", 36, [4, SEQ])
        y_lru = Split("y_lru", 4, Q_AT + 24 * KB)
        y_diff = Split("y_diff", 4, Q_AT + 32 * KB)
        y_win = Split("y_win", 4, Q_AT + 40 * KB)
        y_fox = Split("y_fox", 4, R_AT + 40 * KB)

        def keep(b, to, feature_major=True, scale=1.0):
            slot, done = stream_block("w_in", b, lhs, feature_major=4 if feature_major else 0)
            act.wait(done)
            got = []
            for i in range(2):
                o = to[:, 2 * i:2 * i + 2, :] if feature_major else to[:, i, :]
                a = slot.view[:, i, :]
                if feature_major:
                    a = a.rearrange("p (a b) -> p a b", a=2)
                got.append(scaled(o, a, scale))
            slot.users = got
            return got

        got_lx = keep(0, lxT)
        got_lg = keep(1, lgT)

        def log1p(o, e, s, s2, ready):
            dve.wait(*ready)
            t = ts(dve, s2, e, 2.0, ALU.add)
            dve.wait(t)
            t = dve.do(lambda x: x.reciprocal(s2, s2))
            dve.wait(t)
            t = tt(dve, s, e, s2, ALU.mult)
            dve.wait(t)
            t = tt(dve, s2, s, s, ALU.mult)
            dve.wait(t)
            t = ts(dve, o, s2, 1.0 / 17, ALU.mult)
            for k in (15, 13, 11, 9, 7, 5, 3):
                dve.wait(t)
                t = stt(o, o, 1.0 / k, s2, ALU.add, ALU.mult)
            dve.wait(t)
            t = stt(o, o, 1.0, s, ALU.add, ALU.mult)
            dve.wait(t)
            return ts(dve, o, o, 2.0, ALU.mult)

        def lru():
            xc, gate_w = spot("xc", 0, [4, SEQ], Q_AT), spot("lru_gate_w", 4, [8, P], Q_AT)
            decay, drive = spot("decay", 8, [4, SEQ], Q_AT), spot("drive", 12, [4, SEQ], Q_AT)
            work = spot("lru_work", 16, [4, SEQ], Q_AT)
            work2 = spot("lru_work2", 20, [4, SEQ], Q_AT)
            pool.wait(*lhs.tickets(KT - 1))
            w_ready = load(pool, gate_w[:, :, :], dram["lru_gate_w"], "ld_lru_gate_w")
            cols_ready = ld["lru_cols"]
            dve.wait(*got_lx, *got_lg, cols_ready, *lhs.tickets(KT - 1))
            act.wait(*got_lx, cols_ready)
            half_bias = columns(8)
            hb = [ts(dve, half_bias[:, 4 * g:4 * g + 4], lru_cols[:, 5 + g, :], 0.5, ALU.mult) for g in range(2)]
            soft, e, s, s2 = columns(4), columns(4), columns(4), columns(4)
            neg = columns(4)
            t = ts(dve, neg, lru_cols[:, 7, :], -1.0, ALU.mult)
            dve.wait(t)
            t = tt(dve, e, lru_cols[:, 7, :], neg, ALU.min)
            act.wait(t)
            t = activate(e, e, ACT.Exp)
            yield
            t = log1p(soft, e, s, s2, [t])
            dve.wait(t)
            m = ts(dve, neg, neg, 0.0, ALU.max)
            dve.wait(m)
            t = tt(dve, soft, soft, neg, ALU.add)
            dve.wait(t)
            soft_ready = ts(dve, soft, soft, -4.0, ALU.mult)
            yield
            conv = []
            for f in range(4):
                t = ts(dve, xc[:, f, :], lxT[:, f, :], lru_cols[:, 3, f:f + 1], ALU.mult,
                       lru_cols[:, 4, f:f + 1], ALU.add)
                for back in (1, 2, 3):
                    dve.wait(t)
                    t = stt(xc[:, f, back:], lxT[:, f, 0:SEQ - back], lru_cols[:, 3 - back, f:f + 1],
                            xc[:, f, back:], ALU.mult, ALU.add)
                conv.append(t)
                if f % 2:
                    yield
            gates = []
            for g, to in ((0, decay), (1, drive)):
                for pair in range(2):
                    bank = take("misc", misc)
                    pe.wait(w_ready, conv[-1])
                    for f in (0, 1):
                        t = matmul_done(bank.view[:, f * SEQ:(f + 1) * SEQ], gate_w[:, 4 * g + 2 * pair + f, :],
                                        xc[:, 2 * pair + f, :])
                    act.wait(t, *hb)
                    for f in (0, 1):
                        n = 2 * pair + f
                        t = activate(to[:, n, :], bank.view[:, f * SEQ:(f + 1) * SEQ], ACT.Tanh, scale=0.5,
                                     bias=half_bias[:, 4 * g + n:4 * g + n + 1])
                    bank.users = [t]
                    gates.append(t)
                    yield
            dve.wait(*gates, soft_ready)
            for f in range(4):
                la = ts(dve, decay[:, f, :], decay[:, f, :], 1.0, ALU.add, soft[:, f:f + 1], ALU.mult)
            ix = stt(drive[:, :, :], drive[:, :, :], 1.0, xc[:, :, :], ALU.add, ALU.mult)
            act.wait(la)
            t1 = activate(work[:, :, :], decay[:, :, :], ACT.Exp)
            t2 = activate(work2[:, :, :], decay[:, :, :], ACT.Tanh, scale=0.5)
            yield
            dve.wait(t1, t2)
            t = stt(work[:, :, :], work[:, :, :], 1.0, work2[:, :, :], ALU.add, ALU.mult)
            act.wait(t)
            t2 = activate(work2[:, :, :], decay[:, :, :], ACT.Tanh)
            dve.wait(t, t2)
            a = ts(dve, decay[:, :, :], work[:, :, :], 1.0, ALU.add)
            dve.wait(a)
            yield
            t = tt(dve, work[:, :, :], decay[:, :, :], decay[:, :, :], ALU.mult)
            dve.wait(t)
            t = stt(work[:, :, :], work[:, :, :], 1.0, work2[:, :, :], ALU.add, ALU.mult)
            dve.wait(t)
            t = ts(dve, work[:, :, :], work[:, :, :], -1.0, ALU.mult, 2.0 ** -100, ALU.max)
            act.wait(t)
            root = activate(work[:, :, :], work[:, :, :], ACT.Sqrt)
            yield
            dve.wait(t)
            t = tt(dve, work2[:, :, :], lgT[:, :, :], lgT[:, :, :], ALU.mult)
            dve.wait(t)
            t = ts(dve, work2[:, :, :], work2[:, :, :], 0.044715, ALU.mult, 1.0, ALU.add)
            dve.wait(t)
            t = tt(dve, work2[:, :, :], work2[:, :, :], lgT[:, :, :], ALU.mult)
            act.wait(t)
            th = activate(work2[:, :, :], work2[:, :, :], ACT.Tanh, scale=math.sqrt(2 / math.pi))
            yield
            dve.wait(root, ix)
            t = tt(dve, drive[:, :, :], drive[:, :, :], work[:, :, :], ALU.mult)
            dve.wait(t)
            t = ts(dve, drive[:, :, :], drive[:, :, :], 0.5, ALU.mult)
            dve.wait(t, a)
            yield
            for f in range(4):
                scan = dve.do(lambda e, f=f: e.tensor_tensor_scan(
                    work[:, f, :], decay[:, f, :], drive[:, f, :], 0.0, ALU.mult, ALU.add))
            dve.wait(th)
            gel = stt(lgT[:, :, :], work2[:, :, :], 1.0, lgT[:, :, :], ALU.add, ALU.mult)
            dve.wait(scan, gel)
            yield
            t = stt(work[:, :, :], work[:, :, :], 0.5, lgT[:, :, :], ALU.mult, ALU.mult)
            got = split_store([(y_lru.hi[:, :, :], y_lru.lo[:, :, :], work[:, :, :], None)], [t])
            y_lru.wrote(range(4), got)
            yield

        lru_task = lru()
        background.append(lru_task)

        got_aq = keep(2, aqT, scale=64 ** -0.5)
        got_ak = keep(3, akT)
        got_av = keep(4, av, feature_major=False)
        slot, done = stream_block("w_in_misc", 0, lhs, feature_major=2)
        act.wait(done)
        got_dk = scaled(dkT[:, :], slot.view[:, 0, 0:SEQ], 1.0)
        got_cf = scaled(cfT[:, :], slot.view[:, 0, SEQ:2 * SEQ], 1.0)
        got_dv = scaled(dv[:, :, :], slot.view[:, 1, 0:SEQ].rearrange("p (a b) -> p a b", a=2), 1.0)
        slot.users = [got_dv]
        finish(lru_task)

        prob = [Slot(spot(f"prob{i}", 32 + 1.5 * i, [384])) for i in range(2)]
        probT = [Slot(spot(f"probT{i}", 35 + 1.5 * i, [384])) for i in range(2)]
        y_tok = [Slot(spot(f"y_tok{i}", 38 + i, [2, P])) for i in range(2)]
        SPANS = ((0, P), (P, 3 * P))

        def scores(q, k, more=None, ready=()):
            bank = take("misc", misc)
            pe.wait(*ready)
            for qt, (a, b) in enumerate(SPANS):
                o = bank.view[:, a:b]
                terms = [(o, q[:, qt * P:(qt + 1) * P], k[:, 0:b - a])] + (more(o, qt) if more else [])
                for n, (oo, w, x) in enumerate(terms):
                    t = matmul_done(oo, w, x, start=(qt == 0 and n == 0), stop=n == len(terms) - 1)
            return bank, t

        def row_max(o, src, ready):
            dve.wait(*ready)
            for qt, (a, b) in enumerate(SPANS):
                t = dve.do(lambda e, qt=qt, a=a, b=b: e.tensor_reduce(
                    o[:, qt:qt + 1], src[:, a:b], AX, ALU.max, negate=True))
            return t

        def exponents(p, src, neg_max, total, ready):
            act.wait(*ready)
            for qt, (a, b) in enumerate(SPANS):
                t = activate(p[:, a:b], src[:, a:b], ACT.Exp, bias=neg_max[:, qt:qt + 1],
                             accum_out=total[:, qt:qt + 1])
            return t

        def turn_probs(p, pT, ready):
            bank = take("misc", misc)
            pe.wait(*ready)
            done = turn_tiles(bank.view, [p[:, i * P:(i + 1) * P] for i in range(3)])
            dve.wait(done, *pT.users)
            t = dve.do(lambda e: e.tensor_copy(pT.view[:, :], bank.view[:, 0:384]))
            bank.users = [t]
            return t, done

        small4 = columns(16)
        attn_stats = [small4[:, 4 * i:4 * i + 4] for i in range(4)]
        lam_col = columns(1)

        def lam_scalar():
            vec = spot("lam_vec", 36.75, [4, 64])
            t = load(pool, vec[:, :, :].rearrange("p a b -> p (a b)"), dram["lam_vectors"].partition_broadcast(P),
                     "ld_lam")
            e = attn_stats[3]
            dve.wait(t)
            for i in range(2):
                m = tt(dve, vec[:, 2 * i, :], vec[:, 2 * i, :], vec[:, 2 * i + 1, :], ALU.mult)
                dve.wait(m)
                t = dve.do(lambda x, i=i: x.tensor_reduce(e[:, i:i + 1], vec[:, 2 * i, :], AX, ALU.add))
            act.wait(t)
            t = activate(e[:, 0:2], e[:, 0:2], ACT.Exp)
            dve.wait(t)
            t = tt(dve, e[:, 2:3], e[:, 1:2], e[:, 0:1], ALU.subtract)
            dve.wait(t)
            return ts(dve, lam_col, e[:, 2:3], -LAM_INIT, ALU.add)

        def diff_attention():
            pool.wait(*y_lru.tickets(0))
            lam_ready = lam_scalar()
            y_ready_w = []
            g = columns(4)
            sub_gain = g[:, 0:1]
            dve.wait(ld["subln_col"])
            gain_ready = ts(dve, sub_gain, subln_col[:, :], 1.0 - LAM_INIT, ALU.mult)
            yield
            pools = None
            for h in range(4):
                slope = 2.0 ** (-8.0 * (h + 1) / 4)
                e_done = []
                for m in range(2):
                    rows = slice(64 * m, 64 * m + 64)
                    nm, total = attn_stats[m][:, 0:2], attn_stats[m][:, 2:4]
                    p = prob[m]
                    bank, done = scores(aqT[rows, h, :], akT[rows, h, :], ready=[*got_aq, *got_ak])
                    dve.wait(done, ld["c_dist_a"], *p.users, lam_ready)
                    t = stt(p.view[:, :], dist_a[:, :], -slope, bank.view[:, 0:384], ALU.mult, ALU.add)
                    bank.users = [t]
                    t = row_max(nm, p.view, [t])
                    e_done.append(exponents(p.view, p.view, nm, total, [t]))
                    yield
                dve.wait(*e_done)
                r0, r1 = attn_stats[0][:, 2:4], attn_stats[1][:, 2:4]
                t0 = dve.do(lambda e: e.reciprocal(r0, r0))
                t1 = dve.do(lambda e: e.reciprocal(r1, r1))
                dve.wait(t1, lam_ready)
                t1 = ts(dve, r1, r1, lam_col, ALU.mult)
                dve.wait(t0, t1)
                p0, p1 = prob[0].view, prob[1].view
                for qt, (a, b) in enumerate(SPANS):
                    t = ts(dve, p0[:, a:b], p0[:, a:b], r0[:, qt:qt + 1], ALU.mult)
                dve.wait(t)
                for qt, (a, b) in enumerate(SPANS):
                    t = stt(p0[:, a:b], p1[:, a:b], r1[:, qt:qt + 1], p0[:, a:b], ALU.mult, ALU.add)
                prob[1].users = [t]
                yield
                pT = probT[h % 2]
                t, read = turn_probs(p0, pT, [t])
                prob[0].users = [read]
                yield
                bank = take("misc", misc)
                pe.wait(t, *got_av)
                hs = slice(h * P, (h + 1) * P)
                o = bank.view
                matmul(o[:, 0:P], pT.view[:, 0:P], av[:, 0, hs], True, True)
                matmul(o[:, P:2 * P], pT.view[:, P:2 * P], av[:, 0, hs], False, False)
                done = matmul_done(o[:, P:2 * P], pT.view[:, 2 * P:3 * P], av[:, 1, hs], False, True)
                pT.users = [done]
                yield
                y = y_tok[h % 2]
                ss = g[:, 2:4]
                act.wait(done, *y.users)
                if pools:
                    act.wait(pools)
                for qt in range(2):
                    t = square_sum(o[:, qt * P:(qt + 1) * P], ss[:, qt:qt + 1])
                c = scaled(y.view[:, :, :], o[:, 0:SEQ].rearrange("p (a b) -> p a b", a=2), 1.0)
                bank.users = [c]
                root = inverse_root(ss, ss, P, [t])
                yield
                dve.wait(root, c)
                for qt in range(2):
                    pools = t = ts(dve, y.view[:, qt, :], y.view[:, qt, :], ss[:, qt:qt + 1], ALU.mult)
                bank = take("misc", misc)
                pe.wait(t)
                done = turn_tiles(bank.view, [y.view[:, 0, :], y.view[:, 1, :]])
                y.users = [done]
                act.wait(gain_ready)
                bank.users = split_store([(y_diff.hi[:, h, :], y_diff.lo[:, h, :], bank.view[:, 0:SEQ], sub_gain)],
                                         [done])
                y_diff.wrote([h], bank.users)
                yield

        def window_attention():
            neg_sink, es = columns(8), columns(4)
            dve.wait(ld["sinks"])
            ns_ready = ts(dve, neg_sink, sink_rows[:, :], -1.0, ALU.mult)
            for j in range(4):
                pTs = []
                for kv in range(2):
                    n = 4 * kv + j
                    slope = 2.0 ** (-8.0 * (n + 1) / 8)
                    rows = slice(64 * kv, 64 * kv + 64)
                    p, pT = prob[kv], probT[kv]
                    nm, total = attn_stats[kv][:, 0:2], attn_stats[kv][:, 2:4]
                    bank, done = scores(dqT[rows, j, :], dkT[rows, :], ready=[*got_dq, got_dk])
                    dve.wait(done, ld["c_dist_d"], *p.users)
                    t = stt(p.view[:, :], dist_d[:, :], -slope, bank.view[:, 0:384], ALU.mult, ALU.add)
                    bank.users = [t]
                    t = row_max(nm, p.view, [t])
                    dve.wait(t, ns_ready)
                    t = ts(dve, nm, nm, neg_sink[:, n:n + 1], ALU.min)
                    t = exponents(p.view, p.view, nm, total, [t, ns_ready])
                    s = activate(es[:, 2 * kv:2 * kv + 2], nm, ACT.Exp, bias=sink_rows[:, n:n + 1])
                    yield
                    dve.wait(t, s)
                    t = tt(dve, total, total, es[:, 2 * kv:2 * kv + 2], ALU.add)
                    dve.wait(t)
                    t = dve.do(lambda e, total=total: e.reciprocal(total, total))
                    dve.wait(t)
                    for qt, (a, b) in enumerate(SPANS):
                        t = ts(dve, p.view[:, a:b], p.view[:, a:b], total[:, qt:qt + 1], ALU.mult)
                    t, read = turn_probs(p.view, pT, [t])
                    p.users = [read]
                    pTs.append(t)
                    yield
                bank = take("misc", misc)
                pe.wait(*pTs, got_dv)
                for kv in range(2):
                    rows, w = slice(64 * kv, 64 * kv + 64), probT[kv].view
                    vs = slice(64 * kv, 64 * kv + 64)
                    matmul(bank.view[rows, 0:P], dv[:, 0, vs], w[:, 0:P], True, True)
                    matmul(bank.view[rows, P:SEQ], dv[:, 0, vs], w[:, P:2 * P], False, False)
                    done = matmul_done(bank.view[rows, P:SEQ], dv[:, 1, vs], w[:, 2 * P:3 * P], False, True)
                    probT[kv].users = [done]
                bank.users = split_store([(y_win.hi[:, j, :], y_win.lo[:, j, :], bank.view[:, 0:SEQ], None)], [done])
                y_win.wrote([j], bank.users)
                yield

        def forget_attention():
            cum = spot("cum", 0, [4, SEQ])
            neg_cum = spot("neg_cum", 4, [4, SEQ])
            f, e, s, s2 = (neg_cum[0:4, i, :] for i in range(4))
            lf, negf = cum[0:4, 0, :], cum[0:4, 1, :]
            dve.wait(got_cf, ld["fox_bias"], *y_diff.tickets(3), fill_ones, ld["c_onehot4"])
            t = ts(dve, f, cfT[0:4, :], fox_bias[0:4, :], ALU.add)
            dve.wait(t)
            t = ts(dve, negf, f, -1.0, ALU.mult)
            dve.wait(t)
            t = tt(dve, e, f, negf, ALU.min)
            act.wait(t)
            t = activate(e, e, ACT.Exp)
            yield
            t = log1p(lf, e, s, s2, [t])
            yield
            dve.wait(t)
            m = ts(dve, f, f, 0.0, ALU.min)
            dve.wait(m)
            t = tt(dve, f, f, lf, ALU.subtract)
            dve.wait(t)
            t = dve.do(lambda x: x.tensor_tensor_scan(cfT[0:4, :], ones[0:4, :], f, 0.0, ALU.mult, ALU.add))
            dve.wait(t)
            for h in range(4):
                t1 = ts(dve, cum[0:4, h, :], cfT[0:4, :], onehot4[0:4, h:h + 1], ALU.mult)
                t2 = ts(dve, neg_cum[0:4, h, :], cfT[0:4, :], onehot4[0:4, h:h + 1], ALU.mult, -1.0, ALU.mult)
            yield
            for h in range(4):
                p, pT = prob[h % 2], probT[h % 2]
                nm, total = attn_stats[h % 2][:, 0:2], attn_stats[h % 2][:, 2:4]

                def more(o, qt, h=h):
                    n = P * (qt + 1)
                    return [(o, cum[0:4, h, qt * P:(qt + 1) * P], ones[0:4, 0:n]),
                            (o, ones[0:4, 0:P], neg_cum[0:4, h, 0:n]),
                            (o[:, n - P:n], ident[:, :], diag_mask[:, :])]

                bank, done = scores(cqT[:, h, :], ckT[:, h, :], more,
                                    [*got_cq, *got_ck, t1, t2, ld["c_diag_mask"]])
                t = row_max(nm, bank.view, [done])
                act.wait(*p.users)
                t = exponents(p.view, bank.view, nm, total, [t])
                bank.users = [t]
                yield
                dve.wait(t)
                t = dve.do(lambda e, total=total: e.reciprocal(total, total))
                dve.wait(t)
                for qt, (a, b) in enumerate(SPANS):
                    t = ts(dve, p.view[:, a:b], p.view[:, a:b], total[:, qt:qt + 1], ALU.mult)
                t, read = turn_probs(p.view, pT, [t])
                p.users = [read]
                yield
                bank = take("misc", misc)
                pe.wait(t, *got_cv)
                hs = slice(h * P, (h + 1) * P)
                w = pT.view
                matmul(bank.view[:, 0:P], cv[:, 0, hs], w[:, 0:P], True, True)
                matmul(bank.view[:, P:SEQ], cv[:, 0, hs], w[:, P:2 * P], False, False)
                done = matmul_done(bank.view[:, P:SEQ], cv[:, 1, hs], w[:, 2 * P:3 * P], False, True)
                pT.users = [done]
                bank.users = split_store([(y_fox.hi[:, h, :], y_fox.lo[:, h, :], bank.view[:, 0:SEQ], None)], [done])
                y_fox.wrote([h], bank.users)
                yield

        diff_task = diff_attention()
        background.append(diff_task)
        got_dq = keep(5, dqT, scale=64 ** -0.5)
        win_task = window_attention()
        background.append(win_task)
        got_cq = keep(6, cqT, scale=128 ** -0.5)
        got_ck = keep(7, ckT)
        got_cv = keep(8, cv, feature_major=False)
        fox_task = forget_attention()
        background.append(fox_task)

        def mix(suffix, left, branches, mixed, gate_slots, read_gate, after):
            last = {}
            for n, (y, tiles, task) in enumerate(branches):
                for c in range(NB):
                    gate = gate_slots[(n * NB + c) % 2]
                    bias_ready = read_gate.before(n, c, gate)
                    slot, done = stream_block(f"w_gates{suffix}", n * NB + c, left)
                    g_ready = read_gate.evacuate(slot, done, gate, bias_ready)
                    finish(task)
                    slot, done = stream_block(f"w_branch{suffix}{n}", c, y)
                    dve.wait(done, *g_ready)
                    cs = slice(c * BW, (c + 1) * BW)
                    for t in range(2):
                        o = mixed[:, t, cs] if n == 0 else gate.view[:, t, :]
                        m = stt(o, gate.view[:, t, :], 1.0, slot.view[:, t, :], ALU.add, ALU.mult)
                    slot.users = gate.users = [m]
                    if n:
                        dve.wait(m, *last[c])
                        m = tt(dve, mixed[:, :, cs], mixed[:, :, cs], gate.view[:, :, :], ALU.add)
                        gate.users = [m]
                    last[c] = [m]
                    if n == len(branches) - 1:
                        after(c, m)

        gate_slots = [Slot(spot(f"gate{i}", 4 * i, [2, BW], Q_AT)) for i in range(2)]
        mixed = spot("mixed", 8, [2, D], Q_AT)
        bias_port = Port(pool, "bias_landed")

        class BiasedGates:

            def before(self, n, c, gate):
                pool.wait(*gate.users, *y_lru.tickets(0))
                row = dram["b_gate"][0:1, (n * NB + c) * BW:(n * NB + c + 1) * BW]
                return bias_port.move(gate.view[:, 0, :], row.partition_broadcast(P))

            def evacuate(self, slot, done, gate, bias_ready):
                dve.wait(done, bias_ready)
                for t in (1, 0):
                    s = tt(dve, gate.view[:, t, :], slot.view[:, t, :], gate.view[:, 0, :], ALU.add)
                slot.users = [s]
                act.wait(s)
                return [activate(gate.view[:, :, :], gate.view[:, :, :], ACT.Tanh, scale=0.5)]

        def mixed_to_left(left, pending):
            def after(c, m):
                def move():
                    for t in range(2):
                        put_tile_block(left, mixed[:, t, c * BW:(c + 1) * BW], c, t, None, [m])
                        yield
                background.append(move())
            return after

        merged = Split("m", KT, R_AT)
        mix("", lhs, [(y_lru, 4, lru_task), (y_diff, 4, diff_task), (y_win, 4, win_task), (y_fox, 4, fox_task)],
            mixed, gate_slots, BiasedGates(), mixed_to_left(merged, None))

        def residual_blocks(name, left, scale, squares, nxt, gain, extra=None):
            got = []
            for j in range(NB):
                slot, done = stream_block(name, j, left)
                cs = slice(j * BW, (j + 1) * BW)
                dve.wait(done)
                for t in range(2):
                    if scale == 1.0:
                        m = tt(dve, resid[:, t, cs], slot.view[:, t, :], resid[:, t, cs], ALU.add)
                    else:
                        m = stt(resid[:, t, cs], slot.view[:, t, :], scale, resid[:, t, cs], ALU.mult, ALU.add)
                slot.users = [m]
                if squares is not None:
                    act.wait(m)
                    for t in range(2):
                        s = square_sum(resid[:, t, cs], squares[:, NB * t + j:NB * t + j + 1])
                    got.append(s)
                    if nxt is not None:
                        def move(j=j, m=m, cs=cs):
                            for t in range(2):
                                put_tile_block(nxt, resid[:, t, cs], j, t, gain, [m])
                                yield
                        background.append(move())
                if extra:
                    extra(j, m)
            return got

        def row_root(squares, o, ready):
            total = columns(2)
            dve.wait(*ready)
            t = dve.do(lambda e: e.tensor_reduce(total, squares.rearrange("p (t j) -> p t j", j=NB), AX, ALU.add))
            return inverse_root(o, total, D, [t])

        def ffn(names, left, half_r, half_r2, r_ready, squares, nxt, gain, extra=None):
            gate_n, up_n, down_n = names
            block = 0
            for part, blocks in enumerate(FF_PARTS):
                hidden = Split(f"hidden_{down_n}{part}", 4 * FF_PARTS[0], R_AT)
                moves = []
                for j in range(blocks):
                    gslot, gdone = stream_block(gate_n, block + j, left)
                    sig = silu[j % 2]
                    if j >= 2:
                        finish(moves[j - 2])
                    act.wait(gdone, *r_ready, *sig.users)
                    for t in range(2):
                        th = activate(sig.view[:, t, :], gslot.view[:, t, :], ACT.Tanh, scale=half_r[:, t:t + 1])
                    dve.wait(th, *r_ready)
                    for t in range(2):
                        m = stt(sig.view[:, t, :], sig.view[:, t, :], 1.0, gslot.view[:, t, :], ALU.add, ALU.mult)
                    gslot.users = [m]
                    uslot, udone = stream_block(up_n, block + j, left)
                    dve.wait(udone, m)
                    for t in range(2):
                        m = stt(sig.view[:, t, :], sig.view[:, t, :], half_r2[:, t:t + 1], uslot.view[:, t, :],
                                ALU.mult, ALU.mult)
                    uslot.users = [m]

                    def move(j=j, m=m, sig=sig, hidden=hidden):
                        for t in range(2):
                            put_tile_block(hidden, sig.view[:, t, :], j, t, None, [m])
                            if t:
                                sig.users = hidden.ready[4 * j][-1]
                            yield
                    moves.append(move())
                    background.insert(0, moves[-1])
                last = part == len(FF_PARTS) - 1
                ready = residual_blocks(down_n, hidden, 1.0, squares if last else None,
                                        nxt, gain, extra if last else None)
                block += blocks
            return ready

        v_left = Split("v", KT, U_AT)
        squares1 = columns(8)
        ready = residual_blocks("w_out", merged, 0.5, squares1, v_left, gains[:, 1, :])
        silu = [Slot(spot(f"silu{i}", 4 * i, [2, BW], Q_AT)) for i in range(2)]

        def ffn_rows(squares, ready):
            r = columns(2)
            half_r, half_r2 = columns(2), columns(2)
            root = row_root(squares, r, ready)
            dve.wait(root)
            t1 = ts(dve, half_r, r, 0.5, ALU.mult)
            dve.wait(t1)
            t2 = tt(dve, half_r2, r, half_r, ALU.mult)
            return half_r, half_r2, [t1, t2]

        half_r, half_r2, r_ready = ffn_rows(squares1, ready)

        mem_left = Split("mem", KT, Q_AT + 8 * KB)
        mem_blocks = [Slot(spot(f"mem_in{i}", 40 + 2 * i, [BW], Q_AT)) for i in range(2)]
        mem_squares, r_mem = columns(8), columns(2)
        mem_port = [Port(pool, f"mem_landed{i}") for i in range(2)]
        after_mix = merged.tickets(KT - 1)

        def memory_in():
            got = []
            for j in range(NB):
                for t in range(2):
                    b = mem_blocks[(2 * j + t) % 2]
                    pool.wait(*b.users, *after_mix)
                    t_in = mem_port[(2 * j + t) % 2].move(b.view[:, :], dram["mem"][t, :, j * BW:(j + 1) * BW])
                    yield
                    yield
                    act.wait(t_in, *after_mix)
                    s = square_sum(b.view[:, :], mem_squares[:, NB * t + j:NB * t + j + 1])
                    put_tile_block(mem_left, b.view, j, t, gains[:, 5, :], [t_in])
                    b.users = [s, *mem_left.ready[4 * j][-1]]
                    got.append(s)
                    yield
            mem_root.append(row_root(mem_squares, r_mem, got))

        mem_root = []

        gain12 = columns(16)
        dve.wait(gains_ready)
        gain12_ready = tt(dve, gain12, gains[:, 2, :], gains[:, 3, :], ALU.mult)
        mem_task = memory_in()
        u2 = Split("u2", KT, U_AT)
        act.wait(gain12_ready)
        squares2 = columns(8)
        background.append(mem_task)
        ready = ffn(("w_ffn_gate", "w_ffn_up", "w_ffn_down"), v_left, half_r, half_r2, r_ready,
                    squares2, u2, gain12)
        finish(mem_task)
        while background:
            step_background()

        r1, r2, r12 = columns(2), columns(2), columns(2)
        final_row = [Slot(spot(f"final_row{i}", 40 + 2 * i, [BW], Q_AT)) for i in range(2)]
        row_port = [Port(pool, f"final_row_landed{i}") for i in range(2)]
        root = row_root(squares2, r1, ready)

        def block_norm():
            got = []
            u2_read = [t for k in range(KT) for t in u2.tickets(k)]
            for j in range(NB):
                row = final_row[j % 2]
                pool.wait(*row.users, *[t for k in range(KT) for t in mem_left.tickets(k)])
                r_in = row_port[j % 2].move(
                    row.view[:, :], dram["norm_final"][0:1, j * BW:(j + 1) * BW].partition_broadcast(P))
                dve.wait(r_in, root, *u2_read)
                act.wait(*u2_read)
                cs = slice(j * BW, (j + 1) * BW)
                for t in range(2):
                    m = stt(resid[:, t, cs], resid[:, t, cs], r1[:, t:t + 1], row.view[:, :], ALU.mult, ALU.mult)
                row.users = [m]
                act.wait(m)
                for t in range(2):
                    s = square_sum(resid[:, t, cs], squares2[:, NB * t + j:NB * t + j + 1])
                got.append(s)
                yield
            back = row_root(squares2, r2, got)
            dve.wait(back)
            r12_ready.append(tt(dve, r12, r1, r2, ALU.mult))

        r12_ready = []
        norm_task = block_norm()
        background.append(norm_task)

        qaT, kaT, va = spot("qaT", 0, [6, SEQ]), spot("kaT", 6, [6, SEQ]), spot("va", 12, [2, 6 * P])
        qbT, kbT, vb = spot("qbT", 18, [6, SEQ]), spot("kbT", 24, [2, SEQ]), spot("vb", 26, [2, 2 * P])
        qcT, kcT, vc = spot("qcT", 28, [4, SEQ]), spot("kcT", 32, [4, SEQ]), spot("vc", 36, [2, BW])
        stage_m = [Slot(spot(f"stage_m{i}", 44 + 2 * i, [BW], Q_AT)) for i in range(2)]
        stage = [Slot(spot(f"stage{i}", 2 * i, [BW], Q_AT)) for i in range(2)]
        turned = Slot(spot("turned", 4, [BW], Q_AT))
        rope_work = spot("rope_work", 6, [4, 64], Q_AT)
        pool.wait(*y_diff.tickets(3), *y_win.tickets(3))
        tab_ready = [load(pool, rope[:, :, :, :], dram["c_rope"], "ld_rope"),
                     load(pool, head_gain_rows[:, :, :].rearrange("p a b -> p (a b)"),
                          dram["head_gain_rows"].partition_broadcast(P), "ld_head_gain_rows")]
        head_ss = [columns(4), columns(4)]
        gain_col = {}
        scale128 = 128 ** -0.5
        dve.wait(ld["head_gain_cols"])
        q_gain = columns(4)
        q_gain_ready = ts(dve, q_gain, head_gain_cols[:, :], scale128, ALU.mult)
        gain_col = {"qa": q_gain[:, 0:1], "ka": head_gain_cols[:, 1:2], "qc": q_gain[:, 2:3],
                    "kc": head_gain_cols[:, 3:4], "qb": scale128, "kb": 1.0}
        dest = {"qa": qaT, "ka": kaT, "qb": qbT, "kb": kbT, "qc": qcT, "kc": kcT}
        head_ready = {k: [] for k in dest}

        def head_norms(stages, heads, staged):
            rotary = heads[0][0] in ("qb", "kb")
            for t in range(2):
                st, ss = stages[t], head_ss[t]
                v4 = st.view[:, :].rearrange("p (a b) -> p a b", a=4)
                act.wait(staged[t], *turned.users)
                sq = activate(turned.view[:, :], st.view[:, :], ACT.Square)
                dve.wait(sq)
                s = dve.do(lambda e, ss=ss: e.tensor_reduce(
                    ss, turned.view[:, :].rearrange("p (a b) -> p a b", a=4), AX, ALU.add))
                turned.users = [s]
                root = inverse_root(ss, ss, P, [s])
                yield
                dve.wait(root)
                s = tt(dve, v4, v4, ss.unsqueeze(2).to_broadcast([P, 4, P]), ALU.mult)
                src = st
                if rotary:
                    dve.wait(s, *tab_ready)
                    a = 0
                    while a < 4:
                        b = a
                        while b < 4 and heads[b][0] == heads[a][0]:
                            b += 1
                        g = head_gain_rows[:, 0 if heads[a][0] == "qb" else 1, :]
                        s = tt(dve, v4[:, a:b, :], v4[:, a:b, :], g.unsqueeze(1).to_broadcast([P, b - a, P]), ALU.mult)
                        a = b
                    yield
                    pairs = st.view[:, :].rearrange("p (a d two) -> p a d two", a=4, two=2)
                    outs = turned.view[:, :].rearrange("p (a d two) -> p a d two", a=4, two=2)
                    cos = rope[:, 0, t, :].unsqueeze(1).to_broadcast([P, 4, 64])
                    sin = rope[:, 1, t, :].unsqueeze(1).to_broadcast([P, 4, 64])
                    x0, x1 = pairs[:, :, :, 0], pairs[:, :, :, 1]
                    dve.wait(s, *turned.users)
                    m1 = tt(dve, outs[:, :, :, 0], x0, cos, ALU.mult)
                    m2 = tt(dve, rope_work[:, :, :], x1, sin, ALU.mult)
                    dve.wait(m1, m2)
                    m = tt(dve, outs[:, :, :, 0], outs[:, :, :, 0], rope_work[:, :, :], ALU.subtract)
                    m1 = tt(dve, outs[:, :, :, 1], x0, sin, ALU.mult)
                    dve.wait(m)
                    m2 = tt(dve, rope_work[:, :, :], x1, cos, ALU.mult)
                    dve.wait(m1, m2)
                    s = tt(dve, outs[:, :, :, 1], outs[:, :, :, 1], rope_work[:, :, :], ALU.add)
                    st.users = [s]
                    src = turned
                    yield
                bank = take("misc", misc)
                pe.wait(s)
                done = turn_tiles(bank.view, [src.view[:, i * P:(i + 1) * P] for i in range(4)])
                src.users = [done]
                act.wait(done, q_gain_ready, ld["head_gain_cols"])
                a = 0
                while a < 4:
                    b = a
                    while b < 4 and heads[b][0] == heads[a][0]:
                        b += 1
                    kind, first = heads[a]
                    c = scaled(dest[kind][:, first:first + b - a, t * P:(t + 1) * P],
                               bank.view[:, a * P:b * P].rearrange("p (a b) -> p a b", a=b - a), gain_col[kind])
                    head_ready[kind].append(c)
                    a = b
                bank.users = [c]
                yield

        stage_task = {}

        def project_heads(name, b, left, row_scale, ready, stages, heads):
            slot, done = stream_block(name, b, left)
            if stages[0] in stage_task:
                finish(stage_task[stages[0]])
            act.wait(*ready, done)
            staged = []
            for t in range(2):
                act.wait(*stages[t].users)
                staged.append(scaled(stages[t].view[:, :], slot.view[:, t, :], row_scale[:, t:t + 1]))
            slot.users = staged
            task = stage_task[stages[0]] = head_norms(stages, heads, staged)
            background.insert(0, task)
            return task

        def project_values(name, b, left, row_scale, ready, spans):
            slot, done = stream_block(name, b, left)
            act.wait(*ready, done)
            got = []
            for to, c0, b0, n in spans:
                for t in range(2):
                    got.append(scaled(to[:, t, c0:c0 + n], slot.view[:, t, b0:b0 + n], row_scale[:, t:t + 1]))
            slot.users = got
            return got

        kc_task = project_heads("w_mem", 0, mem_left, r_mem, mem_root, stage_m,
                                [("kc", i) for i in range(4)])
        got_vc = project_values("w_mem", 1, mem_left, r_mem, mem_root, [(vc, 0, 0, BW)])
        finish(norm_task)
        finish(kc_task)
        rr = r12_ready
        qc_task = project_heads("w_in2", 0, u2, r12, rr, stage, [("qc", i) for i in range(4)])

        prob2 = [Slot(spot(f"prob2_{i}", 40 + 2 * i, [2, SEQ])) for i in range(2)]
        prob2T = [Slot(spot(f"prob2T_{i}", 44 + 2 * i, [2, SEQ])) for i in range(2)]
        y_cross = Split("y_cross", 4, Q_AT + 36 * KB)
        y_gqa = Split("y_gqa", 6, Q_AT + 24 * KB)
        y_dil = Split("y_dil", 2, Q_AT + 44 * KB)
        stat2 = [columns(4), columns(4)]

        def dense_attention(n_heads, q, k, v, group, y, ready):
            for h in range(n_heads):
                kv = h // group
                p, pT = prob2[h % 2], prob2T[h % 2]
                nm, total = stat2[h % 2][:, 0:2], stat2[h % 2][:, 2:4]
                bank = take("misc", misc)
                pe.wait(*ready())
                for qt in range(2):
                    t = matmul_done(bank.view[:, qt * SEQ:(qt + 1) * SEQ], q[:, h, qt * P:(qt + 1) * P], k[:, kv, :],
                                    start=qt == 0)
                s = bank.view[:, :].rearrange("p (a b) -> p a b", a=2)
                dve.wait(t)
                t = dve.do(lambda e, nm=nm, s=s: e.tensor_reduce(nm, s, AX, ALU.max, negate=True))
                act.wait(t, *p.users)
                for qt in range(2):
                    t = activate(p.view[:, qt, :], s[:, qt, :], ACT.Exp, bias=nm[:, qt:qt + 1],
                                 accum_out=total[:, qt:qt + 1])
                bank.users = [t]
                yield
                dve.wait(t)
                t = dve.do(lambda e, total=total: e.reciprocal(total, total))
                dve.wait(t)
                for qt in range(2):
                    t = ts(dve, p.view[:, qt, :], p.view[:, qt, :], total[:, qt:qt + 1], ALU.mult)
                bank = take("misc", misc)
                pe.wait(t)
                done = turn_tiles(bank.view, [p.view[:, qt, st * P:(st + 1) * P] for st in range(2) for qt in range(2)])
                p.users = [done]
                yield
                act.wait(done, *pT.users)
                t = scaled(pT.view[:, :, :], bank.view[:, :].rearrange("p (a b) -> p a b", a=2), 1.0)
                bank.users = [t]
                bank = take("misc", misc)
                pe.wait(t)
                for st in range(2):
                    done = matmul_done(bank.view[:, 0:SEQ], v[:, st, kv * P:(kv + 1) * P], pT.view[:, st, :],
                                       st == 0, st == 1)
                pT.users = [done]
                yield
                bank.users = split_store([(y.hi[:, h, :], y.lo[:, h, :], bank.view[:, 0:SEQ], None)], [done])
                y.wrote([h], bank.users)
                yield

        cross_task = dense_attention(4, qcT, kcT, vc, 1, y_cross,
                                     lambda: [*head_ready["qc"], *head_ready["kc"], *got_vc])
        background.append(cross_task)
        project_heads("w_in2", 1, u2, r12, rr, stage, [("qb", j) for j in range(4)])
        project_heads("w_in2", 2, u2, r12, rr, stage, [("qb", 4), ("qb", 5), ("kb", 0), ("kb", 1)])
        got_vb = project_values("w_in2", 3, u2, r12, rr, [(vb, 0, 0, 2 * P), (va, 0, 2 * P, 2 * P)])
        gqa_task = dense_attention(6, qbT, kbT, vb, 3, y_gqa,
                                   lambda: [*head_ready["qb"], *head_ready["kb"], *got_vb])
        background.append(gqa_task)
        got_va = got_vb + project_values("w_in2", 4, u2, r12, rr, [(va, 2 * P, 0, BW)])
        heads_a = [("qa", i) for i in range(6)] + [("ka", i) for i in range(6)]
        for g in range(3):
            a_task = project_heads("w_in2", 5 + g, u2, r12, rr, stage, heads_a[4 * g:4 * g + 4])
        finish(a_task)

        toeplitz = dram["scratch_bias"]
        onehots = spot("onehots", 0, [BW], Q_AT)
        rows_out = spot("bias_rows", 2, [BW], Q_AT)
        spread = spot("table_spread", 4, [6, P], Q_AT)

        def bias_table():
            users = [*stage[0].users, *stage[1].users, *turned.users]
            dve.wait(one_row, ld["table"], *users)
            wide = dve.do(lambda e: e.tensor_copy(spread[0:33, :, :],
                                                  table[0:33, :].unsqueeze(2).to_broadcast([33, 6, P])))
            stores, done = [], wide
            for h in range(6):
                if h % 2 == 0:
                    pool.wait(*users, done)
                    t = onehot_port.move(onehots[0:33, :], dram["c_onehots"][h // 2])
                bank = take("misc", misc)
                pe.wait(t, wide)
                done = matmul_done(bank.view[:, :], spread[0:33, h, :], onehots[0:33, :])
                act.wait(done, *users, *stores)
                c = scaled(rows_out[:, :], bank.view[:, :], 1.0)
                bank.users = [c]
                pool.wait(c)
                stores = [store_port.move(toeplitz[h], rows_out[:, :])]
                yield
            table_out.extend(stores)

        onehot_port, store_port = Port(pool, "onehots_landed"), Port(pool, "bias_rows_stored")
        table_out = []
        table_task = bias_table()
        background.append(table_task)
        finish(table_task)

        probd = [Slot(spot(f"probd{i}", 28 + 3 * i, [3, SEQ])) for i in range(2)]
        probdT = [Slot(spot(f"probdT{i}", 34 + 3 * i, [3, 2, P])) for i in range(2)]
        skew_port = [Port(pool, f"bias_landed{i}") for i in range(2)]

        def dilated_attention():
            pool.wait(*y_cross.tickets(3))
            bias_in = {}

            def fetch(i):
                hh, qt = divmod(i, 2)
                p = probd[i % 2]
                pool.wait(*p.users, *table_out)
                for g in range(3):
                    rows = toeplitz[2 * g + hh]
                    skew = bass.AP(rows.tensor, rows.offset + 255 - P * qt, [[BW - 1, P], [1, SEQ]])
                    bias_in[i] = skew_port[i % 2].move(p.view[:, g, :], skew)

            fetch(0)
            yield
            for i in range(4):
                hh, qt = divmod(i, 2)
                p, pT = probd[i % 2], probdT[i % 2]
                if i < 3:
                    fetch(i + 1)
                nm, total = stat2[i % 2][:, 0:1], stat2[i % 2][:, 2:3]
                dve.wait(bias_in[i])
                for g in range(3):
                    bank = take("misc", misc)
                    pe.wait(*head_ready["qa"], *head_ready["ka"])
                    done = matmul_done(bank.view[:, 0:SEQ], qaT[:, 2 * g + hh, qt * P:(qt + 1) * P], kaT[:, 2 * g + hh, :])
                    dve.wait(done)
                    t = tt(dve, p.view[:, g, :], bank.view[:, 0:SEQ], p.view[:, g, :], ALU.add)
                    bank.users = [t]
                    yield
                flat = p.view[:, :, :].rearrange("p a b -> p (a b)")
                dve.wait(t)
                t = dve.do(lambda e, nm=nm, flat=flat: e.tensor_reduce(nm, flat, AX, ALU.max, negate=True))
                act.wait(t)
                t = activate(flat, flat, ACT.Exp, bias=nm, accum_out=total)
                yield
                dve.wait(t)
                t = dve.do(lambda e, total=total: e.reciprocal(total, total))
                dve.wait(t)
                t = ts(dve, flat, flat, total, ALU.mult)
                yield
                for half in range(2):
                    bank = take("misc", misc)
                    pe.wait(t)
                    done = turn_tiles(bank.view, [flat[:, (3 * half + n) * P:(3 * half + n + 1) * P] for n in range(3)])
                    act.wait(done, *pT.users)
                    c = scaled(pT.view[:, :, :, :].rearrange("p a b c -> p (a b c)")[:, 384 * half:384 * (half + 1)],
                               bank.view[:, 0:384], 1.0)
                    bank.users = [c]
                p.users = [done]
                yield
                bank = take("misc", misc)
                pe.wait(c, *got_va)
                for n in range(6):
                    g, st = divmod(n, 2)
                    done = matmul_done(bank.view[:, 0:P], va[:, st, (2 * g + hh) * P:(2 * g + hh + 1) * P],
                                       pT.view[:, g, st, :], n == 0, n == 5)
                pT.users = [done]
                yield
                o = slice(qt * P, (qt + 1) * P)
                bank.users = split_store([(y_dil.hi[:, hh, o], y_dil.lo[:, hh, o], bank.view[:, 0:P], None)], [done])
                y_dil.wrote([hh], bank.users, parts=2)
                yield

        dil_task = dilated_attention()
        background.append(dil_task)

        class ScaledGates:

            def before(self, n, c, gate):
                return None

            def evacuate(self, slot, done, gate, _):
                act.wait(done, *gate.users, half_r12_ready, *gates_free)
                for t in range(2):
                    g = activate(gate.view[:, t, :], slot.view[:, t, :], ACT.Tanh, scale=half_r12[:, t:t + 1])
                slot.users = [g]
                return [g]

        half_r12 = columns(2)
        dve.wait(*r12_ready)
        half_r12_ready = ts(dve, half_r12, r12, 0.5, ALU.mult)
        gates_free = [*table_out]
        for g in gate_slots:
            g.users = []
        merged2 = Split("m2", KT, R_AT)
        mix("2", u2, [(y_cross, 4, cross_task), (y_gqa, 6, gqa_task), (y_dil, 2, dil_task)],
            mixed, gate_slots, ScaledGates(), mixed_to_left(merged2, None))

        v2 = Split("v2", KT, U_AT)
        squares3 = columns(8)
        ready = residual_blocks("w_out2", merged2, 0.5, squares3, v2, gains[:, 4, :])
        for s in silu:
            s.users = []
        half_r, half_r2, r_ready = ffn_rows(squares3, ready)
        stored = []

        def store(j, m):
            sp.wait(m)
            cs = slice(j * BW, (j + 1) * BW)
            for t in range(2):
                stored.append(load(sp, out[t, :, cs], resid[:, t, cs], f"stored{j}_{t}"))

        ffn(("w_ffn_gate2", "w_ffn_up2", "w_ffn_down2"), v2, half_r, half_r2, r_ready, None, None, None, store)
        while background:
            step_background()
        assert stream["half"] == len(halves)
        sp.wait(*stored)

        block = ctx.enter_context(nc.Block())
        block.sync(sp.emit)
        block.gpsimd(pool.emit)
        block.scalar(act.emit)
        block.vector(dve.emit)
        block.tensor(pe.emit)


def blocks(w, width=BW):
    k, n = w.shape
    return np.ascontiguousarray(w.reshape(k // P, P, n // width, width).transpose(2, 1, 0, 3)
                                .reshape(n // width, P, (k // P) * width))


def column(v):
    return np.ascontiguousarray(v.reshape(-1, P).T)


def constants():
    pos = np.arange(P, dtype=np.float32)
    diff = pos[:, None] - pos[None, :]
    far = np.float32(1e32)
    diag = np.where(diff >= 0, diff, far).astype(np.float32)
    off = diff + P
    band = np.where(off < 128, off, far).astype(np.float32)
    n = np.abs(np.arange(-255, 257))
    rel = np.arange(-255, 257)
    nb, exact = 16, 8
    large = exact + (np.log(np.maximum(n, 1).astype(np.float32) / exact)
                     / math.log(1024 / exact) * (nb - exact)).astype(np.int32)
    bucket = np.where(rel > 0, nb, 0) + np.where(n < exact, n, np.minimum(large, nb - 1))
    onehots = np.zeros((3, 33, 512), np.float32)
    for g, dil in enumerate((1, 4, 16)):
        valid = (rel % dil == 0) & (n // dil <= 64)
        for i in np.nonzero(valid)[0]:
            onehots[g, bucket[i], i] = 1.0
        onehots[g, 32] = np.where(valid, 0.0, MASKED)
    inv = 10000.0 ** (-np.arange(32, dtype=np.float32) / 32)
    tok = np.arange(SEQ)
    ang = np.concatenate([(tok // 64).astype(np.float32)[:, None] * inv,
                          (tok % 64).astype(np.float32)[:, None] * inv], axis=-1).astype(np.float32)
    rope = np.stack([np.cos(ang), np.sin(ang)]).astype(np.float32).reshape(2, 2, P, 64).transpose(2, 0, 1, 3)
    return {
        "c_ident": np.eye(P, dtype=np.float32),
        "c_diag_mask": np.where(diff >= 0, 0.0, MASKED).astype(np.float32),
        "c_dist_a": np.concatenate([diag, off, diag], 1).astype(np.float32),
        "c_dist_d": np.concatenate([diag, band, diag], 1).astype(np.float32),
        "c_onehot4": np.eye(4, dtype=np.float32),
        "c_onehots": onehots,
        "c_rope": np.ascontiguousarray(rope),
    }


def lay_out(i):
    w = i["w_in"][0]
    at = np.cumsum((0, 512, 512, 512, 512, 512, 512, 512, 512, 4, 512, 128, 128, 8192))
    aq, ak, av, bx, bg, cq, ck, cv, cf, dq, dk, dv, gz = (w[:, a:b] for a, b in zip(at[:-1], at[1:]))
    pair = np.concatenate([np.r_[64 * j:64 * j + 64, 256 + 64 * j:256 + 64 * j + 64] for j in range(4)])
    a = {}
    a["w_in"] = blocks(np.concatenate([bx, bg, aq, ak, av, dq[:, pair], cq, ck, cv], 1))
    a["w_in_misc"] = blocks(np.concatenate([dk, cf, np.zeros((D, 124), np.float32), dv], 1), 384)
    order = (1, 0, 3, 2)
    a["w_gates"] = blocks(np.concatenate([gz[:, n * D:(n + 1) * D] for n in order], 1))
    a["b_gate"] = np.concatenate([i["b_gate"][:, n * D:(n + 1) * D] for n in order], 1)
    for k, n in enumerate(order):
        wb = i["w_branch"][0, n]
        a[f"w_branch{k}"] = blocks(wb[pair] if n == 3 else wb)
    a["w_out"] = blocks(i["w_out"][0])
    a["w_ffn_gate"], a["w_ffn_up"] = blocks(i["w_ffn_gate"][0]), blocks(i["w_ffn_up"][0])
    a["w_ffn_down"] = blocks(i["w_ffn_down"][0])
    a["x"] = i["x"].reshape(2, P, D)
    a["mem"] = i["mem_2"].reshape(2, P, D)
    a["gains"] = np.stack([column(i[n].reshape(-1)) for n in
                           ("norm_mix", "norm_ffn", "norm_final", "g_mix_2", "g_ffn_2", "g_mem_2")], 1)
    a["norm_final"] = i["norm_final"].reshape(1, D)
    a["lru_cols"] = np.stack([column(i["lru_conv_w"][0, j]) for j in range(4)] +
                             [column(i[n][0]) for n in ("lru_conv_b", "lru_ba", "lru_bx", "lru_lambda")], 1)
    diag = np.zeros((2, 4, P, P), np.float32)
    for g, n in enumerate(("lru_wa", "lru_wx")):
        for b in range(8):
            s = slice(64 * (b % 2), 64 * (b % 2) + 64)
            diag[g, b // 2, s, s] = i[n][0, b]
    a["lru_gate_w"] = diag.reshape(8, P, P).transpose(1, 0, 2)
    a["lam_vectors"] = np.concatenate([i[n] for n in ("diff_lq1", "diff_lk1", "diff_lq2", "diff_lk2")], 1)
    a["subln_col"] = i["diff_subln"].reshape(P, 1)
    a["fox_bias"] = i["fox_b_f"].reshape(4, 1)
    a["sinks"] = i["swa_sinks"].reshape(1, 8)
    w = i["w_in_2"][0]
    at = np.cumsum((0, 768, 768, 768, 768, 256, 256, 512, 6144))
    qa, ka, va, qb, kb, vb, qc, gz = (w[:, x:y] for x, y in zip(at[:-1], at[1:]))
    a["w_in2"] = blocks(np.concatenate([qc, qb, kb, vb, va, qa, ka], 1))
    order = (2, 1, 0)
    a["w_gates2"] = blocks(np.concatenate([gz[:, n * D:(n + 1) * D] for n in order], 1))
    for k, n in enumerate(("w_br_c_2", "w_br_b_2", "w_br_a_2")):
        a[f"w_branch2{k}"] = blocks(i[n][0])
    a["w_mem"] = blocks(i["w_mem_kv_2"][0])
    a["w_out2"] = blocks(i["w_o_2"][0])
    a["w_ffn_gate2"] = blocks(i["w_ffn_in_2"][0][:, :D_FF])
    a["w_ffn_up2"] = blocks(i["w_ffn_in_2"][0][:, D_FF:])
    a["w_ffn_down2"] = blocks(i["w_ffn_out_2"][0])
    a["head_gain_cols"] = np.stack([i[n].reshape(P) for n in ("g_qa_2", "g_ka_2", "g_qc_2", "g_kc_2")], 1)
    a["head_gain_rows"] = np.concatenate([i["g_qb_2"], i["g_kb_2"]], 1)
    a["table"] = i["rel_bias_2"]
    a.update(constants())
    return {n: np.ascontiguousarray(v) for n, v in a.items()}


def kernel(**inputs):
    import concourse.bacc as bacc
    from concourse.bass_utils import run_bass_kernel_spmd

    arrays = lay_out({n: np.asarray(v) for n, v in inputs.items()})
    nc = bacc.Bacc("TRN2", target_bir_lowering=False, num_devices=1)
    dram = {n: nc.dram_tensor(f"in_{n}", v.shape, mybir.dt.from_np(v.dtype), kind="ExternalInput").ap()
            for n, v in arrays.items()}
    dram["scratch_bias"] = nc.dram_tensor("scratch_bias", (6, P, BW), F32, kind="Internal").ap()
    out = nc.dram_tensor("out_tokens", (2, P, D), F32, kind="ExternalOutput").ap()
    build(nc, dram, out)
    got = run_bass_kernel_spmd(nc, [{f"in_{n}": v for n, v in arrays.items()}], core_ids=[0])
    return got.results[0]["out_tokens"].reshape(1, SEQ, D)
```

```python
import math
from contextlib import ExitStack

import numpy as np

import concourse.bass as bass
from concourse import mybir

F32 = mybir.dt.float32
F32R = mybir.dt.float32r
BF16 = mybir.dt.bfloat16
ALU = mybir.AluOpType
ACT = mybir.ActivationFunctionType
AX = mybir.AxisListType.X

P = 128
SEQ = 256
D = 2048
KT = D // P
BW = 512
NB = D // BW
D_FF = 5632
FF_PARTS = (6, 5)
CHUNK_KT = 4
HALF_KT = 2
RAW_SLOTS, PART_SLOTS = 3, 4
AHEAD = 3
EPS = 1e-6
LAM_INIT = 0.8 - 0.6 * math.exp(0.0)
MASKED = -1e30
KB = 1024


class Line:

    def __init__(self, sem):
        self.sem, self.count, self.queue, self.seen = sem, 0, [], {}

    def wait(self, *tickets):
        for sem, value in tickets:
            if self.seen.get(sem.name, 0) < value:
                self.seen[sem.name] = value
                self.queue.append(lambda e, s=sem, v=value: e.wait_ge(s, v))

    def run(self, instruction):
        self.queue.append(instruction)

    def do(self, instruction):
        self.count += 1
        self.queue.append(lambda e: instruction(e).then_inc(self.sem, 1))
        return (self.sem, self.count)

    def emit(self, engine):
        for instruction in self.queue:
            instruction(engine)


class Slot:

    def __init__(self, view):
        self.view, self._users, self.held = view, [], False

    @property
    def users(self):
        return self._users

    @users.setter
    def users(self, tickets):
        self._users, self.held = tickets, False


def weight_plan():
    plan = [("w_in", b, 0, KT, BW) for b in range(5)]
    plan += [("w_in_misc", 0, 0, KT, P + 4 + P)]
    plan += [("w_in", b, 0, KT, BW) for b in range(5, 9)]
    for n in range(4):
        for c in range(NB):
            plan += [("w_gates", n * NB + c, 0, KT, BW), (f"w_branch{n}", c, 0, 4, BW)]
    plan += [("w_out", b, 0, KT, BW) for b in range(NB)]

    def ffn(gate, up, down):
        out, block = [], 0
        for part in FF_PARTS:
            for b in range(block, block + part):
                out += [(gate, b, 0, KT, BW), (up, b, 0, KT, BW)]
            out += [(down, b, 4 * block, 4 * part, BW) for b in range(NB)]
            block += part
        return out

    plan += ffn("w_ffn_gate", "w_ffn_up", "w_ffn_down")
    plan += [("w_mem", b, 0, KT, BW) for b in range(2)]
    plan += [("w_in2", b, 0, KT, BW) for b in range(8)]
    for n, tiles in enumerate((4, 6, 2)):
        for c in range(NB):
            plan += [("w_gates2", n * NB + c, 0, KT, BW), (f"w_branch2{n}", c, 0, tiles, BW)]
    plan += [("w_out2", b, 0, KT, BW) for b in range(NB)]
    plan += ffn("w_ffn_gate2", "w_ffn_up2", "w_ffn_down2")
    return plan


def build(nc, dram, out):
    ctx = ExitStack()
    with ctx:
        sem_of = {n: ctx.enter_context(nc.semaphore(f"done_{n}")) for n in ("pe", "act", "dve", "pool")}
        pe, act, dve, pool = (Line(sem_of[n]) for n in ("pe", "act", "dve", "pool"))
        sp = Line(None)
        raw_landed = [ctx.enter_context(nc.semaphore(f"raw_landed{i}")) for i in range(RAW_SLOTS)]

        def load(line, to, of, sem_name):
            sem = ctx.enter_context(nc.semaphore(sem_name))
            line.run(lambda e: e.dma_start(to, of).then_inc(sem, 16))
            return (sem, 16)

        class Port:

            def __init__(self, line, name):
                self.line, self.n = line, 0
                self.sem = ctx.enter_context(nc.semaphore(name))

            def move(self, to, of):
                if self.n:
                    self.line.wait((self.sem, 16 * self.n))
                self.n += 1
                self.line.run(lambda e: e.dma_start(to, of).then_inc(self.sem, 16))
                return (self.sem, 16 * self.n)

        at = [(nc.sbuf_base + 31) // 32 * 32]

        def region(size):
            at[0] += size
            return at[0] - size

        def place(name, shape, dtype, offset):
            return nc.alloc_sbuf_tensor_at(name, [P, *shape], dtype, offset=offset)

        X_AT, RAW_AT = region(16 * KB), region(RAW_SLOTS * 8 * KB)
        HI_AT, LO_AT = region(PART_SLOTS * 4 * KB), region(PART_SLOTS * 4 * KB)
        U_AT, R_AT, Q_AT = region(32 * KB), region(48 * KB), region(48 * KB)

        resid = place("resid", [2, D], F32, X_AT)
        raw = place("raw", [RAW_SLOTS, CHUNK_KT * BW], F32, RAW_AT)
        w_hi = place("w_hi", [PART_SLOTS, HALF_KT * BW], F32R, HI_AT)
        w_lo = place("w_lo", [PART_SLOTS, HALF_KT * BW], F32R, LO_AT)

        class Split:

            def __init__(self, name, tiles, offset):
                self.hi = place(f"{name}_hi", [tiles, SEQ], F32R, offset)
                self.lo = place(f"{name}_lo", [tiles, SEQ], F32R, offset + tiles * KB)
                self.ready = {}

            def wrote(self, tiles, tickets, parts=1):
                for k in tiles:
                    self.ready.setdefault(k, []).append(tickets)
                    self.parts = parts

            def tickets(self, k):
                while len(self.ready.get(k, ())) < self.parts_of(k):
                    assert movers or tasks, "a left operand that nobody writes"
                    step_background()
                return [t for group in self.ready[k] for t in group]

            def parts_of(self, k):
                return self.parts if k in self.ready else 1

        def small(name, shape, dtype=F32):
            size = int(np.prod(shape)) * (4 if dtype != BF16 else 2)
            return place(name, shape, dtype, region((size + 31) // 32 * 32))

        ident = small("ident", [P])
        diag_mask = small("diag_mask", [P])
        ones = small("ones", [SEQ])
        junk = small("junk", [BW], BF16)
        gains = small("gains", [6, KT])
        lru_cols = small("lru_cols", [8, 4])
        stats = small("stats", [192])
        tab1_at = region(3 * KB)
        dist_a = place("dist_a", [384], F32, tab1_at)
        dist_d = place("dist_d", [384], F32, tab1_at + 1536)
        rope = place("rope", [2, 2, 64], F32, tab1_at)
        head_gain_rows = place("head_gain_rows", [2, P], F32, tab1_at + KB)
        subln_col = small("subln_col", [1])
        head_gain_cols = small("head_gain_cols", [4])
        fox_bias = small("fox_bias", [1])
        fox_select = small("fox_select", [10])
        sink_rows = small("sink_rows", [8])
        table = small("table", [6])
        minus_half = small("minus_half", [16])
        assert at[0] <= nc.sbuf_usable_end, (at[0], nc.sbuf_usable_end)

        acc = [Slot(ctx.enter_context(nc.psum_tensor(f"acc{i}", [P, 2, BW], F32))) for i in range(2)]
        misc = [Slot(ctx.enter_context(nc.psum_tensor(f"misc{i}", [P, BW], F32))) for i in range(4)]
        turn = {"acc": 0, "misc": 0}

        def take(kind, slots):
            while slots[turn[kind] % len(slots)].held:
                turn[kind] += 1
            slot = slots[turn[kind] % len(slots)]
            turn[kind] += 1
            pe.wait(*slot.users)
            slot.held = True
            return slot

        def matmul(o, w, x, start=True, stop=True):
            pe.run(lambda e: e.matmul(o, w, x, start=start, stop=stop, skip_group_check=True))

        def matmul_done(o, w, x, start=True, stop=True):
            return pe.do(lambda e: e.matmul(o, w, x, start=start, stop=stop, skip_group_check=True))

        def turn_tiles(o, tiles):
            for i, tile in enumerate(tiles):
                go = pe.do if i == len(tiles) - 1 else pe.run
                ticket = go(lambda e, i=i, tile=tile: e.transpose(o[:, i * P:(i + 1) * P], tile, ident[:, :]))
            return ticket

        def tt(line, o, a, b, op):
            return line.do(lambda e: e.tensor_tensor(o, a, b, op))

        def ts(line, o, a, s1, op0, s2=None, op1=None):
            if op1 is None:
                return line.do(lambda e: e.tensor_scalar(o, a, s1, None, op0))
            return line.do(lambda e: e.tensor_scalar(o, a, s1, s2, op0, op1))

        def stt(o, a, s, b, op0, op1):
            return dve.do(lambda e: e.scalar_tensor_tensor(o, a, s, b, op0, op1))

        def activate(o, a, func, **kw):
            return act.do(lambda e: e.activation(o, a, func, **kw))

        def scaled(o, a, scale):
            return activate(o, a, ACT.Copy, scale=scale)

        def split_store(pieces, ready):
            act.wait(*ready)
            for o_hi, _, a, scale in pieces:
                hi = activate(o_hi, a, ACT.Copy, **({} if scale is None else {"scale": scale}))
            dve.wait(*ready, hi)
            for o_hi, o_lo, a, scale in pieces:
                if scale is None:
                    lo = tt(dve, o_lo, a, o_hi.bitcast(F32), ALU.subtract)
                else:
                    lo = stt(o_lo, a, scale, o_hi.bitcast(F32), ALU.mult, ALU.subtract)
            return [hi, lo]

        used_stats = [0]

        def columns(n):
            used_stats[0] += n
            assert used_stats[0] <= 192
            return stats[:, used_stats[0] - n:used_stats[0]]

        junk_written = []

        def square_sum(a, o, ready=()):
            act.wait(*ready, *junk_written)
            junk_written[:] = [activate(junk[:, 0:a.shape[1]], a, ACT.Square, accum_out=o)]
            return junk_written[0]

        def inverse_root(o, squares, n, ready):
            pool.wait(*ready)
            t = ts(pool, o, squares, 1.0 / n, ALU.mult, EPS, ALU.add)
            pool.wait(t)
            return tt(pool, o, o, minus_half[:, 0:o.shape[1]], ALU.pow)

        def row_root(squares, o, ready):
            total = columns(2)
            dve.wait(*ready)
            t = dve.do(lambda e: e.tensor_reduce(total, squares.rearrange("p (t j) -> p t j", j=NB), AX, ALU.add))
            return inverse_root(o, total, D, [t])

        ident_ready = load(act, ident[:, :], dram["c_ident"], "ld_ident")
        gains_ready = load(act, gains[:, :, :], dram["gains"], "ld_gains")
        fill_ones = pool.do(lambda e: e.memset(ones[:, :], 1.0))
        fill_half = pool.do(lambda e: e.memset(minus_half[:, :], -0.5))
        pool.wait(fill_half)
        act.wait(fill_half)
        scaled(junk[:, 0:16], minus_half[:, :], 1.0)
        one_row = pool.do(lambda e: e.memset(table[32:33, :], 1.0))
        pool.wait(one_row)

        plan = weight_plan()
        halves = []
        chunks = []
        for name, b, k0, kn, cols in plan:
            for k in range(k0, k0 + kn, CHUNK_KT):
                n = min(CHUNK_KT, k0 + kn - k)
                halves += [(len(chunks), o, HALF_KT, cols) for o in range(0, n, HALF_KT)]
                chunks.append((name, b, k, n, cols))
        stream = {"loaded": 0, "split": 0, "half": 0, "block": 0}
        split_done = {}
        half_read = {}
        last_split = {}
        raw_loads = [0] * RAW_SLOTS
        raw_ticket = {}

        def load_next_chunk():
            c = stream["loaded"]
            if c >= len(chunks):
                return
            name, b, k, n, cols = chunks[c]
            slot = c % RAW_SLOTS
            if c >= RAW_SLOTS:
                sp.wait(*last_split[c - RAW_SLOTS])
            raw_loads[slot] += 1
            raw_ticket[c] = (raw_landed[slot], 16 * raw_loads[slot])
            to, of = raw[:, slot, 0:n * cols], dram[name][b, :, k * cols:(k + n) * cols]
            sp.run(lambda e: e.dma_start(to, of).then_inc(raw_landed[slot], 16))
            stream["loaded"] += 1

        def split_next_half():
            h = stream["split"]
            c, o, n, cols = halves[h]
            slot = h % PART_SLOTS
            a = raw[:, c % RAW_SLOTS, o * cols:(o + n) * cols]
            hi, lo = w_hi[:, slot, 0:n * cols], w_lo[:, slot, 0:n * cols]
            act.wait(raw_ticket[c])
            if h >= PART_SLOTS:
                act.wait(half_read[h - PART_SLOTS])
            t_hi = activate(hi, a, ACT.Copy)
            dve.wait(raw_ticket[c], t_hi)
            t_lo = tt(dve, lo, a, hi.bitcast(F32), ALU.subtract)
            split_done[h] = [t_hi, t_lo]
            if h + 1 == len(halves) or halves[h + 1][0] != c:
                last_split[c] = [t_hi, t_lo]
                load_next_chunk()
            stream["split"] += 1

        def split_ahead(h):
            while stream["split"] < min(h + AHEAD + 1, len(halves)):
                split_next_half()

        movers, tasks = [], []

        def step_background():
            for lane in (movers, tasks):
                while lane and not lane[0].gi_running:
                    try:
                        next(lane[0])
                        break
                    except StopIteration:
                        lane.pop(0)

        def soon(task):
            tasks.insert(0, task)

        def finish(task):
            while task in movers or task in tasks:
                step_background()

        def stream_block(name, b, left, feature_major=0):
            want, kb, k0, kn, cols = plan[stream["block"]]
            assert (want, kb) == (name, b), (want, kb, name, b)
            stream["block"] += 1
            slot = take("acc", acc)
            v = slot.view
            for j in range(kn // HALF_KT):
                h = stream["half"]
                split_ahead(h)
                pe.wait(*split_done[h])
                hi, lo = w_hi[:, h % PART_SLOTS, :], w_lo[:, h % PART_SLOTS, :]
                for i in range(HALF_KT):
                    kt = HALF_KT * j + i
                    first, last = kt == 0, kt == kn - 1
                    pe.wait(*left.tickets(kt))
                    whi = hi[:, i * cols:(i + 1) * cols]
                    wlo = lo[:, i * cols:(i + 1) * cols]
                    lhi, llo = left.hi[:, kt, :], left.lo[:, kt, :]
                    work = []
                    for f in range(feature_major):
                        o = v[:, f // 2, (f % 2) * SEQ:(f % 2 + 1) * SEQ]
                        fs = slice(f * P, (f + 1) * P)
                        work += [(o, whi[:, fs], lhi, f % 2 == 0), (o, whi[:, fs], llo, False),
                                 (o, wlo[:, fs], lhi, False)]
                    done = feature_major * P
                    if done < cols:
                        for t in range(2):
                            ts_ = slice(t * P, (t + 1) * P)
                            o = v[:, t, 0:cols] if not done else v[:, 1, t * (cols - done):(t + 1) * (cols - done)]
                            clears = not done or t == 0
                            work += [(o, lhi[:, ts_], whi[:, done:cols], clears),
                                     (o, lhi[:, ts_], wlo[:, done:cols], False),
                                     (o, llo[:, ts_], whi[:, done:cols], False)]
                    for n, (o, w, x, clears) in enumerate(work):
                        if i == HALF_KT - 1 and n == len(work) - 1:
                            half_read[h] = matmul_done(o, w, x, first and clears, last)
                        else:
                            matmul(o, w, x, first and clears, last)
                stream["half"] += 1
                step_background()
            return slot, half_read[stream["half"] - 1]

        def put_tile_block(left, src, j, t, gain, ready):
            bank = take("misc", misc)
            pe.wait(*ready, ident_ready)
            done = turn_tiles(bank.view, [src[:, i * P:(i + 1) * P] for i in range(4)])
            o = slice(t * P, (t + 1) * P)
            if gain is None:
                pieces = [(left.hi[:, 4 * j:4 * j + 4, o], left.lo[:, 4 * j:4 * j + 4, o],
                           bank.view[:, :].rearrange("p (a b) -> p a b", a=4), None)]
            else:
                pieces = [(left.hi[:, k, o], left.lo[:, k, o], bank.view[:, (k - 4 * j) * P:(k - 4 * j + 1) * P],
                           gain[:, k:k + 1]) for k in range(4 * j, 4 * j + 4)]
                act.wait(gains_ready)
                dve.wait(gains_ready)
            bank.users = split_store(pieces, [done])
            left.wrote(range(4 * j, 4 * j + 4), bank.users, parts=2)

        lhs = Split("u", KT, U_AT)
        x_ready = {}
        for j in range(NB):
            for t in range(2):
                cs = slice(j * BW, (j + 1) * BW)
                x_ready[t, j] = load(sp, resid[:, t, cs], dram["x"][t, :, cs], f"ld_x{t}_{j}")
            if j < RAW_SLOTS:
                load_next_chunk()
        ld = {}
        for n, v in (("c_diag_mask", diag_mask[:, :]), ("c_dist_a", dist_a[:, :]), ("c_dist_d", dist_d[:, :]),
                     ("lru_cols", lru_cols[:, :, :]), ("subln_col", subln_col[:, :]),
                     ("head_gain_cols", head_gain_cols[:, :]), ("fox_bias", fox_bias[0:36, :]),
                     ("c_fox_select", fox_select[0:36, :]), ("table", table[0:32, :])):
            ld[n] = load(pool, v, dram[n], f"ld_{n}")
        ld["sinks"] = load(pool, sink_rows[:, :], dram["sinks"].partition_broadcast(P), "ld_sinks")

        squares0, r_mix = columns(8), columns(2)
        diag_r = place("diag_r", [2, P], F32, Q_AT)
        r_rows = place("r_rows", [SEQ], F32, Q_AT + KB)

        def first_rows():
            got = []
            yield
            for j in range(NB):
                yield
                for t in range(2):
                    got.append(square_sum(resid[:, t, j * BW:(j + 1) * BW], squares0[:, NB * t + j:NB * t + j + 1],
                                          [x_ready[t, j]]))
            yield
            root = row_root(squares0, r_mix, got)
            yield
            dve.wait(root, ident_ready)
            for t in range(2):
                m = ts(dve, diag_r[:, t, :], ident[:, :], r_mix[:, t:t + 1], ALU.mult)
            yield
            bank = take("misc", misc)
            pe.wait(m, fill_ones)
            for t in range(2):
                done = matmul_done(bank.view[:, t * P:(t + 1) * P], ones[:, 0:P], diag_r[:, t, :], start=t == 0)
            act.wait(done)
            bank.users = [scaled(r_rows[:, :], bank.view[:, 0:SEQ], 1.0)]
            r_ready0.extend([root, *bank.users])

        r_ready0 = []
        for j in range(NB):
            def move(j=j):
                for t in range(2):
                    put_tile_block(lhs, resid[:, t, j * BW:(j + 1) * BW], j, t, gains[:, 0, :], [x_ready[t, j]])
                yield
            movers.append(move())
        rows_task = first_rows()
        tasks.append(rows_task)
        step_background()

        def spot(name, kb, shape, base=R_AT, dtype=F32):
            return place(name, shape, dtype, base + int(kb * KB))

        aqT, akT, av = spot("aqT", 0, [4, SEQ]), spot("akT", 4, [4, SEQ]), spot("av", 8, [2, BW])
        dqT, cqT, ckT = spot("dqT", 12, [4, SEQ]), spot("cqT", 16, [4, SEQ]), spot("ckT", 20, [4, SEQ])
        cv, dkT, cfT = spot("cv", 24, [2, BW]), spot("dkT", 28, [SEQ]), spot("cfT", 29, [SEQ])
        cf_tok = spot("cf_tok", 31, [2, 36])
        cf_zeros = pool.do(lambda e: e.memset(cf_tok[:, :, :], 0.0))
        dv = spot("dv", 30, [2, P])
        lxT, lgT = spot("lxT", 32, [4, SEQ]), spot("lgT", 36, [4, SEQ])
        y_lru = Split("y_lru", 4, Q_AT + 24 * KB)
        y_diff = Split("y_diff", 4, Q_AT + 32 * KB)
        y_win = Split("y_win", 4, Q_AT + 40 * KB)
        y_fox = Split("y_fox", 4, R_AT + 40 * KB)

        def keep(b, to, feature_major=True, scale=1.0):
            slot, done = stream_block("w_in", b, lhs, feature_major=4 if feature_major else 0)
            finish(rows_task)
            got = []
            for i in range(2):
                if feature_major:
                    dve.wait(done, *r_ready0)
                    got.append(stt(to[:, 2 * i:2 * i + 2, :], slot.view[:, i, :].rearrange("p (a b) -> p a b", a=2),
                                   scale, r_rows[:, :].unsqueeze(1).to_broadcast([P, 2, SEQ]), ALU.mult, ALU.mult))
                else:
                    act.wait(done, *r_ready0)
                    got.append(scaled(to[:, i, :], slot.view[:, i, :], r_mix[:, i:i + 1]))
            slot.users = got
            return got

        got_lx = keep(0, lxT)
        got_lg = keep(1, lgT)

        def log1p(o, e, s, s2, ready):
            dve.wait(*ready)
            t = ts(dve, s2, e, 2.0, ALU.add)
            dve.wait(t)
            t = dve.do(lambda x: x.reciprocal(s2, s2))
            dve.wait(t)
            t = tt(dve, s, e, s2, ALU.mult)
            yield
            dve.wait(t)
            t = tt(dve, s2, s, s, ALU.mult)
            dve.wait(t)
            t = ts(dve, o, s2, 1.0 / 17, ALU.mult)
            for k in (15, 13, 11, 9, 7, 5, 3):
                if k in (13, 7):
                    yield
                dve.wait(t)
                t = stt(o, o, 1.0 / k, s2, ALU.add, ALU.mult)
            yield
            dve.wait(t)
            t = stt(o, o, 1.0, s, ALU.add, ALU.mult)
            dve.wait(t)
            return ts(dve, o, o, 2.0, ALU.mult)

        def lru():
            xc, gate_w = spot("xc", 0, [4, SEQ], Q_AT + 24 * KB), spot("lru_gate_w", 4, [8, P], Q_AT)
            decay, drive = spot("decay", 8, [4, SEQ], Q_AT), spot("drive", 12, [4, SEQ], Q_AT)
            work = spot("lru_work", 16, [4, SEQ], Q_AT)
            work2 = spot("lru_work2", 20, [4, SEQ], Q_AT)
            w_ready = load(pool, gate_w[:, :, :], dram["lru_gate_w"], "ld_lru_gate_w")
            cols_ready = ld["lru_cols"]
            dve.wait(*got_lx, *got_lg, cols_ready)
            act.wait(*got_lx, cols_ready)
            half_bias = columns(8)
            hb = [ts(dve, half_bias[:, 4 * g:4 * g + 4], lru_cols[:, 5 + g, :], 0.5, ALU.mult) for g in range(2)]
            soft, e, s, s2 = columns(4), columns(4), columns(4), columns(4)
            neg = columns(4)
            t = ts(dve, neg, lru_cols[:, 7, :], -1.0, ALU.mult)
            dve.wait(t)
            t = tt(dve, e, lru_cols[:, 7, :], neg, ALU.min)
            act.wait(t)
            t = activate(e, e, ACT.Exp)
            yield
            t = yield from log1p(soft, e, s, s2, [t])
            dve.wait(t)
            m = ts(dve, neg, neg, 0.0, ALU.max)
            dve.wait(m)
            t = tt(dve, soft, soft, neg, ALU.add)
            dve.wait(t)
            soft_ready = ts(dve, soft, soft, -4.0, ALU.mult)
            yield
            conv = []
            for f in range(4):
                t = ts(dve, xc[:, f, :], lxT[:, f, :], lru_cols[:, 3, f:f + 1], ALU.mult,
                       lru_cols[:, 4, f:f + 1], ALU.add)
                for back in (1, 2, 3):
                    dve.wait(t)
                    t = stt(xc[:, f, back:], lxT[:, f, 0:SEQ - back], lru_cols[:, 3 - back, f:f + 1],
                            xc[:, f, back:], ALU.mult, ALU.add)
                    if back == 2:
                        yield
                conv.append(t)
            yield
            gates = []
            for g, to in ((0, decay), (1, drive)):
                for pair in range(2):
                    bank = take("misc", misc)
                    pe.wait(w_ready, conv[-1])
                    for f in (0, 1):
                        t = matmul_done(bank.view[:, f * SEQ:(f + 1) * SEQ], gate_w[:, 4 * g + 2 * pair + f, :],
                                        xc[:, 2 * pair + f, :])
                    act.wait(t, *hb)
                    for f in (0, 1):
                        n = 2 * pair + f
                        t = activate(to[:, n, :], bank.view[:, f * SEQ:(f + 1) * SEQ], ACT.Tanh, scale=0.5,
                                     bias=half_bias[:, 4 * g + n:4 * g + n + 1])
                    bank.users = [t]
                    gates.append(t)
                    yield
            dve.wait(*gates, soft_ready)
            for f in range(4):
                la = ts(dve, decay[:, f, :], decay[:, f, :], 1.0, ALU.add, soft[:, f:f + 1], ALU.mult)
            yield
            ix = stt(drive[:, :, :], drive[:, :, :], 1.0, xc[:, :, :], ALU.add, ALU.mult)
            act.wait(la)
            t1 = activate(work[:, :, :], decay[:, :, :], ACT.Exp)
            yield
            t2 = activate(work2[:, :, :], decay[:, :, :], ACT.Tanh, scale=0.5)
            yield
            dve.wait(t1, t2)
            t = stt(work[:, :, :], work[:, :, :], 1.0, work2[:, :, :], ALU.add, ALU.mult)
            yield
            act.wait(t)
            t2 = activate(work2[:, :, :], decay[:, :, :], ACT.Tanh)
            yield
            dve.wait(t, t2)
            a = ts(dve, decay[:, :, :], work[:, :, :], 1.0, ALU.add)
            dve.wait(a)
            yield
            t = tt(dve, work[:, :, :], decay[:, :, :], decay[:, :, :], ALU.mult)
            dve.wait(t)
            yield
            t = stt(work[:, :, :], work[:, :, :], 1.0, work2[:, :, :], ALU.add, ALU.mult)
            dve.wait(t)
            yield
            t = ts(dve, work[:, :, :], work[:, :, :], -1.0, ALU.mult, 2.0 ** -100, ALU.max)
            yield
            act.wait(t)
            root = activate(work[:, :, :], work[:, :, :], ACT.Sqrt)
            dve.wait(t)
            t = tt(dve, work2[:, :, :], lgT[:, :, :], lgT[:, :, :], ALU.mult)
            dve.wait(t)
            yield
            t = ts(dve, work2[:, :, :], work2[:, :, :], 0.044715, ALU.mult, 1.0, ALU.add)
            dve.wait(t)
            yield
            t = tt(dve, work2[:, :, :], work2[:, :, :], lgT[:, :, :], ALU.mult)
            yield
            act.wait(t)
            th = activate(work2[:, :, :], work2[:, :, :], ACT.Tanh, scale=math.sqrt(2 / math.pi))
            yield
            dve.wait(root, ix)
            t = tt(dve, drive[:, :, :], drive[:, :, :], work[:, :, :], ALU.mult)
            dve.wait(t)
            yield
            t = ts(dve, drive[:, :, :], drive[:, :, :], 0.5, ALU.mult)
            dve.wait(t, a)
            yield
            for f in range(4):
                scan = dve.do(lambda e, f=f: e.tensor_tensor_scan(
                    work[:, f, :], decay[:, f, :], drive[:, f, :], 0.0, ALU.mult, ALU.add))
                if f % 2:
                    yield
            dve.wait(th)
            gel = stt(lgT[:, :, :], work2[:, :, :], 1.0, lgT[:, :, :], ALU.add, ALU.mult)
            dve.wait(scan, gel)
            yield
            t = stt(work[:, :, :], work[:, :, :], 0.5, lgT[:, :, :], ALU.mult, ALU.mult)
            yield
            got = split_store([(y_lru.hi[:, :, :], y_lru.lo[:, :, :], work[:, :, :], None)], [t])
            y_lru.wrote(range(4), got)
            yield

        lru_task = lru()
        tasks.append(lru_task)

        got_aq = keep(2, aqT, scale=64 ** -0.5)
        got_ak = keep(3, akT)
        got_av = keep(4, av, feature_major=False)
        slot, done = stream_block("w_in_misc", 0, lhs, feature_major=1)
        dve.wait(done, *r_ready0)
        act.wait(done, *r_ready0, cf_zeros)
        got_dk = tt(dve, dkT[:, :], slot.view[:, 0, 0:SEQ], r_rows[:, :], ALU.mult)
        for t in range(2):
            c = slot.view[:, 1, t * (4 + P):(t + 1) * (4 + P)]
            for o in (cf_tok[:, t, 0:4], cf_tok[:, t, 32:36]):
                got_cf = scaled(o, c[:, 0:4], r_mix[:, t:t + 1])
            got_dv = scaled(dv[:, t, :], c[:, 4:4 + P], r_mix[:, t:t + 1])
        slot.users = [got_dk, got_dv]

        prob = [Slot(spot(f"prob{i}", 32 + 1.5 * i, [384])) for i in range(2)]
        probT = [Slot(spot(f"probT{i}", 35 + 1.5 * i, [384])) for i in range(2)]
        y_tok = [Slot(spot(f"y_tok{i}", 38 + i, [2, P])) for i in range(2)]
        SPANS = ((0, P), (P, 3 * P))

        def scores(q, k, more=None, ready=()):
            bank = take("misc", misc)
            pe.wait(*ready)
            for qt, (a, b) in enumerate(SPANS):
                o = bank.view[:, a:b]
                terms = [(o, q[:, qt * P:(qt + 1) * P], k[:, 0:b - a])] + (more(o, qt) if more else [])
                for n, (oo, w, x) in enumerate(terms):
                    t = matmul_done(oo, w, x, start=(qt == 0 and n == 0), stop=n == len(terms) - 1)
            return bank, t

        def row_max(o, src, ready):
            dve.wait(*ready)
            for qt, (a, b) in enumerate(SPANS):
                t = dve.do(lambda e, qt=qt, a=a, b=b: e.tensor_reduce(
                    o[:, qt:qt + 1], src[:, a:b], AX, ALU.max, negate=True))
            return t

        def exponents(p, src, neg_max, total, ready):
            act.wait(*ready)
            for qt, (a, b) in enumerate(SPANS):
                t = activate(p[:, a:b], src[:, a:b], ACT.Exp, bias=neg_max[:, qt:qt + 1],
                             accum_out=total[:, qt:qt + 1])
            return t

        def turn_probs(p, pT, ready):
            bank = take("misc", misc)
            pe.wait(*ready)
            done = turn_tiles(bank.view, [p[:, i * P:(i + 1) * P] for i in range(3)])
            dve.wait(done, *pT.users)
            t = dve.do(lambda e: e.tensor_copy(pT.view[:, :], bank.view[:, 0:384]))
            bank.users = [t]
            return t, done

        small4 = columns(16)
        attn_stats = [small4[:, 4 * i:4 * i + 4] for i in range(4)]
        lam_col = columns(1)

        def lam_scalar():
            vec = spot("lam_vec", 36.75, [4, 64])
            t = load(pool, vec[:, :, :].rearrange("p a b -> p (a b)"), dram["lam_vectors"].partition_broadcast(P),
                     "ld_lam")
            e = attn_stats[3]
            dve.wait(t)
            for i in range(2):
                m = tt(dve, vec[:, 2 * i, :], vec[:, 2 * i, :], vec[:, 2 * i + 1, :], ALU.mult)
                dve.wait(m)
                t = dve.do(lambda x, i=i: x.tensor_reduce(e[:, i:i + 1], vec[:, 2 * i, :], AX, ALU.add))
            act.wait(t)
            t = activate(e[:, 0:2], e[:, 0:2], ACT.Exp)
            dve.wait(t)
            t = tt(dve, e[:, 2:3], e[:, 1:2], e[:, 0:1], ALU.subtract)
            dve.wait(t)
            return ts(dve, lam_col, e[:, 2:3], -LAM_INIT, ALU.add)

        def diff_attention():
            pool.wait(*y_lru.tickets(0))
            lam_ready = lam_scalar()
            g = columns(4)
            sub_gain = g[:, 0:1]
            dve.wait(ld["subln_col"])
            gain_ready = ts(dve, sub_gain, subln_col[:, :], 1.0 - LAM_INIT, ALU.mult)
            yield
            pools = None
            for h in range(4):
                slope = 2.0 ** (-8.0 * (h + 1) / 4)
                e_done = []
                for m in range(2):
                    rows = slice(64 * m, 64 * m + 64)
                    nm, total = attn_stats[m][:, 0:2], attn_stats[m][:, 2:4]
                    p = prob[m]
                    bank, done = scores(aqT[rows, h, :], akT[rows, h, :], ready=[*got_aq, *got_ak])
                    dve.wait(done, ld["c_dist_a"], *p.users, lam_ready)
                    t = stt(p.view[:, :], dist_a[:, :], -slope, bank.view[:, 0:384], ALU.mult, ALU.add)
                    bank.users = [t]
                    t = row_max(nm, p.view, [t])
                    yield
                    e_done.append(exponents(p.view, p.view, nm, total, [t]))
                yield
                dve.wait(*e_done)
                r0, r1 = attn_stats[0][:, 2:4], attn_stats[1][:, 2:4]
                t0 = dve.do(lambda e: e.reciprocal(r0, r0))
                t1 = dve.do(lambda e: e.reciprocal(r1, r1))
                dve.wait(t1, lam_ready)
                t1 = ts(dve, r1, r1, lam_col, ALU.mult)
                dve.wait(t0, t1)
                p0, p1 = prob[0].view, prob[1].view
                for qt, (a, b) in enumerate(SPANS):
                    t = ts(dve, p0[:, a:b], p0[:, a:b], r0[:, qt:qt + 1], ALU.mult)
                yield
                dve.wait(t)
                for qt, (a, b) in enumerate(SPANS):
                    t = stt(p0[:, a:b], p1[:, a:b], r1[:, qt:qt + 1], p0[:, a:b], ALU.mult, ALU.add)
                prob[1].users = [t]
                yield
                pT = probT[h % 2]
                t, read = turn_probs(p0, pT, [t])
                prob[0].users = [read]
                yield
                bank = take("misc", misc)
                pe.wait(t, *got_av)
                hs = slice(h * P, (h + 1) * P)
                o = bank.view
                matmul(o[:, 0:P], pT.view[:, 0:P], av[:, 0, hs], True, True)
                matmul(o[:, P:2 * P], pT.view[:, P:2 * P], av[:, 0, hs], False, False)
                done = matmul_done(o[:, P:2 * P], pT.view[:, 2 * P:3 * P], av[:, 1, hs], False, True)
                pT.users = [done]
                yield
                y = y_tok[h % 2]
                ss = g[:, 2:4]
                act.wait(done, *y.users)
                if pools:
                    act.wait(pools)
                for qt in range(2):
                    t = square_sum(o[:, qt * P:(qt + 1) * P], ss[:, qt:qt + 1])
                c = scaled(y.view[:, :, :], o[:, 0:SEQ].rearrange("p (a b) -> p a b", a=2), 1.0)
                bank.users = [c]
                root = inverse_root(ss, ss, P, [t])
                yield
                dve.wait(root, c)
                for qt in range(2):
                    pools = t = ts(dve, y.view[:, qt, :], y.view[:, qt, :], ss[:, qt:qt + 1], ALU.mult)
                yield
                bank = take("misc", misc)
                pe.wait(t)
                done = turn_tiles(bank.view, [y.view[:, 0, :], y.view[:, 1, :]])
                y.users = [done]
                act.wait(gain_ready)
                bank.users = split_store([(y_diff.hi[:, h, :], y_diff.lo[:, h, :], bank.view[:, 0:SEQ], sub_gain)],
                                         [done])
                y_diff.wrote([h], bank.users)
                yield

        def window_attention():
            neg_sink, es = columns(8), columns(4)
            dve.wait(ld["sinks"])
            ns_ready = ts(dve, neg_sink, sink_rows[:, :], -1.0, ALU.mult)
            for j in range(4):
                pTs = []
                for kv in range(2):
                    n = 4 * kv + j
                    slope = 2.0 ** (-8.0 * (n + 1) / 8)
                    rows = slice(64 * kv, 64 * kv + 64)
                    p, pT = prob[kv], probT[kv]
                    nm, total = attn_stats[kv][:, 0:2], attn_stats[kv][:, 2:4]
                    bank, done = scores(dqT[rows, j, :], dkT[rows, :], ready=[*got_dq, got_dk])
                    dve.wait(done, ld["c_dist_d"], *p.users)
                    t = stt(p.view[:, :], dist_d[:, :], -slope, bank.view[:, 0:384], ALU.mult, ALU.add)
                    bank.users = [t]
                    t = row_max(nm, p.view, [t])
                    dve.wait(t, ns_ready)
                    t = ts(dve, nm, nm, neg_sink[:, n:n + 1], ALU.min)
                    yield
                    t = exponents(p.view, p.view, nm, total, [t, ns_ready])
                    s = activate(es[:, 2 * kv:2 * kv + 2], nm, ACT.Exp, bias=sink_rows[:, n:n + 1])
                    yield
                    dve.wait(t, s)
                    t = tt(dve, total, total, es[:, 2 * kv:2 * kv + 2], ALU.add)
                    dve.wait(t)
                    t = dve.do(lambda e, total=total: e.reciprocal(total, total))
                    yield
                    act.wait(t)
                    for qt, (a, b) in enumerate(SPANS):
                        t = scaled(p.view[:, a:b], p.view[:, a:b], total[:, qt:qt + 1])
                    yield
                    t, read = turn_probs(p.view, pT, [t])
                    p.users = [read]
                    pTs.append(t)
                    yield
                bank = take("misc", misc)
                pe.wait(*pTs, got_dv)
                for kv in range(2):
                    rows, w = slice(64 * kv, 64 * kv + 64), probT[kv].view
                    vs = slice(64 * kv, 64 * kv + 64)
                    matmul(bank.view[rows, 0:P], dv[:, 0, vs], w[:, 0:P], True, True)
                    matmul(bank.view[rows, P:SEQ], dv[:, 0, vs], w[:, P:2 * P], False, False)
                    done = matmul_done(bank.view[rows, P:SEQ], dv[:, 1, vs], w[:, 2 * P:3 * P], False, True)
                    probT[kv].users = [done]
                bank.users = split_store([(y_win.hi[:, j, :], y_win.lo[:, j, :], bank.view[:, 0:SEQ], None)], [done])
                y_win.wrote([j], bank.users)
                yield

        def forget_attention():
            rows = slice(0, 36)
            q_sums, k_sums = spot("q_sums", 0, [4, SEQ]), spot("k_sums", 4, [4, SEQ])
            f, e, s, s2 = (k_sums[rows, i, :] for i in range(4))
            lf, negf = q_sums[rows, 0, :], q_sums[rows, 1, :]
            bank = take("misc", misc)
            pe.wait(got_cf, ident_ready)
            for t in range(2):
                done = pe.do(lambda x, t=t: x.transpose(
                    bank.view[rows, t * P:(t + 1) * P], cf_tok[:, t, :], ident[:, :]))
            dve.wait(done, ld["fox_bias"], *y_diff.tickets(3), fill_ones, ld["c_fox_select"])
            t = ts(dve, f, bank.view[rows, 0:SEQ], fox_bias[rows, :], ALU.add)
            bank.users = [t]
            yield
            dve.wait(t)
            t = ts(dve, negf, f, -1.0, ALU.mult)
            dve.wait(t)
            t = tt(dve, e, f, negf, ALU.min)
            yield
            act.wait(t)
            t = activate(e, e, ACT.Exp)
            yield
            t = yield from log1p(lf, e, s, s2, [t])
            yield
            dve.wait(t)
            m = ts(dve, f, f, 0.0, ALU.min)
            dve.wait(m)
            t = tt(dve, f, f, lf, ALU.subtract)
            dve.wait(t)
            t = dve.do(lambda x: x.tensor_tensor_scan(cfT[rows, :], ones[rows, :], f, 0.0, ALU.mult, ALU.add))
            yield
            dve.wait(t)
            for h in range(4):
                t1 = ts(dve, q_sums[rows, h, :], cfT[rows, :], fox_select[rows, h:h + 1], ALU.mult,
                        fox_select[rows, 8:9], ALU.add)
                t2 = ts(dve, k_sums[rows, h, :], cfT[rows, :], fox_select[rows, 4 + h:5 + h], ALU.mult,
                        fox_select[rows, 9:10], ALU.add)
                if h % 2:
                    yield
            for h in range(4):
                p, pT = prob[h % 2], probT[h % 2]
                nm, total = attn_stats[h % 2][:, 0:2], attn_stats[h % 2][:, 2:4]

                def more(o, qt, h=h):
                    n = P * (qt + 1)
                    return [(o, q_sums[rows, h, qt * P:(qt + 1) * P], k_sums[rows, h, 0:n]),
                            (o[:, n - P:n], ident[:, :], diag_mask[:, :])]

                bank, done = scores(cqT[:, h, :], ckT[:, h, :], more,
                                    [*got_cq, *got_ck, t1, t2, ld["c_diag_mask"]])
                t = row_max(nm, bank.view, [done])
                yield
                act.wait(*p.users)
                t = exponents(p.view, bank.view, nm, total, [t])
                bank.users = [t]
                yield
                dve.wait(t)
                t = dve.do(lambda e, total=total: e.reciprocal(total, total))
                yield
                act.wait(t)
                for qt, (a, b) in enumerate(SPANS):
                    t = scaled(p.view[:, a:b], p.view[:, a:b], total[:, qt:qt + 1])
                yield
                t, read = turn_probs(p.view, pT, [t])
                p.users = [read]
                yield
                bank = take("misc", misc)
                pe.wait(t, *got_cv)
                hs = slice(h * P, (h + 1) * P)
                w = pT.view
                matmul(bank.view[:, 0:P], cv[:, 0, hs], w[:, 0:P], True, True)
                matmul(bank.view[:, P:SEQ], cv[:, 0, hs], w[:, P:2 * P], False, False)
                done = matmul_done(bank.view[:, P:SEQ], cv[:, 1, hs], w[:, 2 * P:3 * P], False, True)
                pT.users = [done]
                bank.users = split_store([(y_fox.hi[:, h, :], y_fox.lo[:, h, :], bank.view[:, 0:SEQ], None)], [done])
                y_fox.wrote([h], bank.users)
                yield

        diff_task = diff_attention()
        tasks.append(diff_task)
        got_dq = keep(5, dqT, scale=64 ** -0.5)
        win_task = window_attention()
        tasks.append(win_task)
        got_cq = keep(6, cqT, scale=128 ** -0.5)
        got_ck = keep(7, ckT)
        got_cv = keep(8, cv, feature_major=False)
        fox_task = forget_attention()
        tasks.append(fox_task)

        def mix(suffix, left, branches, mixed, gate_slots, read_gate, after):
            last = {}
            for n, (y, tiles, task) in enumerate(branches):
                for c in range(NB):
                    gate = gate_slots[(n * NB + c) % 2]
                    bias_ready = read_gate.before(n, c, gate)
                    slot, done = stream_block(f"w_gates{suffix}", n * NB + c, left)
                    g_ready = read_gate.evacuate(slot, done, gate, bias_ready)
                    finish(task)
                    slot, done = stream_block(f"w_branch{suffix}{n}", c, y)
                    dve.wait(done, *g_ready)
                    cs = slice(c * BW, (c + 1) * BW)
                    for t in range(2):
                        o = mixed[:, t, cs] if n == 0 else gate.view[:, t, :]
                        m = stt(o, gate.view[:, t, :], 1.0, slot.view[:, t, :], ALU.add, ALU.mult)
                    slot.users = gate.users = [m]
                    if n:
                        dve.wait(m, *last[c])
                        m = tt(dve, mixed[:, :, cs], mixed[:, :, cs], gate.view[:, :, :], ALU.add)
                        gate.users = [m]
                    last[c] = [m]
                    if n == len(branches) - 1:
                        after(c, m)

        gate_slots = [Slot(spot(f"gate{i}", 4 * i, [2, BW], Q_AT)) for i in range(2)]
        mixed = spot("mixed", 8, [2, D], Q_AT)
        bias_port = Port(pool, "bias_landed")

        class BiasedGates:

            def before(self, n, c, gate):
                pool.wait(*gate.users, *y_lru.tickets(0), *got_ck, got_dk)
                row = dram["b_gate"][0:1, (n * NB + c) * BW:(n * NB + c + 1) * BW]
                return bias_port.move(gate.view[:, 0, :], row.partition_broadcast(P))

            def evacuate(self, slot, done, gate, bias_ready):
                dve.wait(done, bias_ready)
                for t in (1, 0):
                    s = stt(gate.view[:, t, :], slot.view[:, t, :], r_mix[:, t:t + 1], gate.view[:, 0, :],
                            ALU.mult, ALU.add)
                slot.users = [s]
                got = []

                def tanh():
                    act.wait(s)
                    got.append(activate(gate.view[:, :, :], gate.view[:, :, :], ACT.Tanh, scale=0.5))
                    yield
                soon(tanh())
                return got

        def mixed_to_left(left):
            def after(c, m):
                def move():
                    yield
                    for t in range(2):
                        put_tile_block(left, mixed[:, t, c * BW:(c + 1) * BW], c, t, None, [m])
                        yield
                movers.append(move())
            return after

        merged = Split("m", KT, R_AT)
        mix("", lhs, [(y_lru, 4, lru_task), (y_diff, 4, diff_task), (y_win, 4, win_task), (y_fox, 4, fox_task)],
            mixed, gate_slots, BiasedGates(), mixed_to_left(merged))

        def residual_blocks(name, left, scale, squares, nxt, gain, extra=None):
            got = []
            for j in range(NB):
                slot, done = stream_block(name, j, left)
                cs = slice(j * BW, (j + 1) * BW)
                dve.wait(done)
                for t in range(2):
                    if scale == 1.0:
                        m = tt(dve, resid[:, t, cs], slot.view[:, t, :], resid[:, t, cs], ALU.add)
                    else:
                        m = stt(resid[:, t, cs], slot.view[:, t, :], scale, resid[:, t, cs], ALU.mult, ALU.add)
                    if extra:
                        extra(j, t, m)
                slot.users = [m]
                if squares is not None:
                    def sums(j=j, m=m, cs=cs):
                        for t in range(2):
                            got.append(square_sum(resid[:, t, cs], squares[:, NB * t + j:NB * t + j + 1], [m]))
                        yield
                    soon(sums())
                    if nxt is not None:
                        def move(j=j, m=m, cs=cs):
                            for t in range(2):
                                put_tile_block(nxt, resid[:, t, cs], j, t, gain, [m])
                                yield
                        movers.append(move())
            return got

        def ffn(names, left, half_r, half_r2, r_ready, squares, nxt, gain, extra=None):
            gate_n, up_n, down_n = names
            block = 0
            for part, blocks in enumerate(FF_PARTS):
                hidden = Split(f"hidden_{down_n}{part}", 4 * FF_PARTS[0], R_AT)
                moves = []
                for j in range(blocks):
                    gslot, gdone = stream_block(gate_n, block + j, left)
                    sig = silu[j % 2]
                    assert r_ready
                    if j >= 2:
                        finish(moves[j - 2])
                    act.wait(gdone, *r_ready, *sig.users)
                    for t in range(2):
                        th = activate(sig.view[:, t, :], gslot.view[:, t, :], ACT.Tanh, scale=half_r[:, t:t + 1])
                    dve.wait(th, *r_ready)
                    for t in range(2):
                        m = stt(sig.view[:, t, :], sig.view[:, t, :], 1.0, gslot.view[:, t, :], ALU.add, ALU.mult)
                    gslot.users = [m]
                    uslot, udone = stream_block(up_n, block + j, left)
                    dve.wait(udone, m)
                    for t in range(2):
                        m = stt(sig.view[:, t, :], sig.view[:, t, :], half_r2[:, t:t + 1], uslot.view[:, t, :],
                                ALU.mult, ALU.mult)
                    uslot.users = [m]

                    def move(j=j, m=m, sig=sig, hidden=hidden):
                        for t in range(2):
                            put_tile_block(hidden, sig.view[:, t, :], j, t, None, [m])
                            if t:
                                sig.users = hidden.ready[4 * j][-1]
                            yield
                    moves.append(move())
                    movers.append(moves[-1])
                last = part == len(FF_PARTS) - 1
                ready = residual_blocks(down_n, hidden, 1.0, squares if last else None,
                                        nxt, gain, extra if last else None)
                block += blocks
            return ready

        v_left = Split("v", KT, U_AT)
        squares1 = columns(8)
        ready = residual_blocks("w_out", merged, 0.5, squares1, v_left, gains[:, 1, :])
        silu = [Slot(spot(f"silu{i}", 4 * i, [2, BW], Q_AT)) for i in range(2)]

        def ffn_rows(squares, ready):
            r, half_r, half_r2, done = columns(2), columns(2), columns(2), []

            def rows():
                assert len(ready) == 2 * NB
                root = row_root(squares, r, ready)
                yield
                dve.wait(root)
                t1 = ts(dve, half_r, r, 0.5, ALU.mult)
                dve.wait(t1)
                done.extend([t1, tt(dve, half_r2, r, half_r, ALU.mult)])
            tasks.insert(1, rows())
            return half_r, half_r2, done

        half_r, half_r2, r_ready = ffn_rows(squares1, ready)

        mem_left = Split("mem", KT, Q_AT + 8 * KB)
        mem_blocks = [Slot(spot(f"mem_in{i}", 40 + 2 * i, [BW], Q_AT)) for i in range(2)]
        mem_squares, r_mem = columns(8), columns(2)
        mem_port = [Port(pool, f"mem_landed{i}") for i in range(2)]
        after_mix = merged.tickets(KT - 1)

        def memory_in():
            got = []
            for j in range(NB):
                for t in range(2):
                    b = mem_blocks[(2 * j + t) % 2]
                    pool.wait(*b.users, *after_mix)
                    t_in = mem_port[(2 * j + t) % 2].move(b.view[:, :], dram["mem"][t, :, j * BW:(j + 1) * BW])
                    for _ in range(4):
                        yield
                    act.wait(t_in, *after_mix)
                    s = square_sum(b.view[:, :], mem_squares[:, NB * t + j:NB * t + j + 1])
                    put_tile_block(mem_left, b.view, j, t, gains[:, 5, :], [t_in])
                    b.users = [s, *mem_left.ready[4 * j][-1]]
                    got.append(s)
                    yield
            mem_root.append(row_root(mem_squares, r_mem, got))

        mem_root = []

        gain12 = columns(16)
        dve.wait(gains_ready)
        gain12_ready = tt(dve, gain12, gains[:, 2, :], gains[:, 3, :], ALU.mult)

        toeplitz = dram["scratch_bias"]
        onehots, rows_out = spot("onehots", 44, [BW], Q_AT), spot("bias_rows", 46, [BW], Q_AT)
        spread = place("table_spread", [6, P], F32, tab1_at)
        onehot_port, store_port = Port(pool, "onehots_landed"), Port(pool, "bias_rows_stored")
        table_out, spread_read = [], []

        def bias_table():
            dve.wait(one_row, ld["table"], *y_diff.tickets(3), *y_win.tickets(3))
            wide = dve.do(lambda e: e.tensor_copy(spread[0:33, :, :],
                                                  table[0:33, :].unsqueeze(2).to_broadcast([33, 6, P])))
            done = None
            for h in range(6):
                if h % 2 == 0:
                    pool.wait(*([done] if done else after_mix))
                    t = onehot_port.move(onehots[0:33, :], dram["c_onehots"][h // 2])
                    yield
                    yield
                bank = take("misc", misc)
                pe.wait(t, wide)
                done = matmul_done(bank.view[:, :], spread[0:33, h, :], onehots[0:33, :])
                act.wait(done, *after_mix, *table_out[-1:])
                c = scaled(rows_out[:, :], bank.view[:, :], 1.0)
                bank.users = [c]
                pool.wait(c)
                table_out.append(store_port.move(toeplitz[h], rows_out[:, :]))
                yield
                yield
            spread_read.append(done)

        final_row = [Slot(spot(f"final_row{i}", 40 + 2 * i, [BW], Q_AT)) for i in range(2)]
        row_port = [Port(pool, f"final_row_landed{i}") for i in range(2)]
        row_in = {}

        def fetch_row(j):
            if j < NB:
                pool.wait(*final_row[j % 2].users, *mem_left.tickets(KT - 1))
                row_in[j] = row_port[j % 2].move(
                    final_row[j % 2].view[:, :],
                    dram["norm_final"][0:1, j * BW:(j + 1) * BW].partition_broadcast(P))

        def first_row_loads():
            fetch_row(0)
            fetch_row(1)
            yield

        mem_task, table_task = memory_in(), bias_table()
        u2 = Split("u2", KT, U_AT)
        act.wait(gain12_ready)
        squares2 = columns(8)
        tasks.extend([mem_task, first_row_loads(), table_task])
        ready = ffn(("w_ffn_gate", "w_ffn_up", "w_ffn_down"), v_left, half_r, half_r2, r_ready,
                    squares2, u2, gain12)
        finish(table_task)

        r1, r2, r12 = columns(2), columns(2), columns(2)

        def block_norm():
            assert len(ready) == 2 * NB
            root = row_root(squares2, r1, ready)
            yield
            got = []
            u2_read = [t for k in range(KT) for t in u2.tickets(k)]
            for j in range(NB):
                row = final_row[j % 2]
                dve.wait(row_in[j], root, *u2_read)
                act.wait(*u2_read)
                cs = slice(j * BW, (j + 1) * BW)
                for t in range(2):
                    m = stt(resid[:, t, cs], resid[:, t, cs], r1[:, t:t + 1], row.view[:, :], ALU.mult, ALU.mult)
                row.users = [m]
                fetch_row(j + 2)
                yield
                for t in range(2):
                    s = square_sum(resid[:, t, cs], squares2[:, NB * t + j:NB * t + j + 1], [m])
                got.append(s)
            yield
            back = row_root(squares2, r2, got)
            yield
            dve.wait(back)
            r12_ready.append(tt(dve, r12, r1, r2, ALU.mult))

        r12_ready = []
        norm_task = block_norm()
        movers.append(norm_task)

        qaT, kaT, va = spot("qaT", 0, [6, SEQ]), spot("kaT", 6, [6, SEQ]), spot("va", 12, [2, 6 * P])
        qbT, kbT, vb = spot("qbT", 18, [6, SEQ]), spot("kbT", 24, [2, SEQ]), spot("vb", 26, [2, 2 * P])
        qcT, kcT, vc = spot("qcT", 28, [4, SEQ]), spot("kcT", 32, [4, SEQ]), spot("vc", 36, [2, BW])
        stage_m = [Slot(spot(f"stage_m{i}", 44 + 2 * i, [BW], Q_AT)) for i in range(2)]
        stage = [Slot(spot(f"stage{i}", 2 * i, [BW], Q_AT)) for i in range(2)]
        turned = Slot(spot("turned", 4, [BW], Q_AT))
        rope_work = spot("rope_work", 6, [4, 64], Q_AT)
        pool.wait(*spread_read)
        tab_ready = [load(pool, rope[:, :, :, :], dram["c_rope"], "ld_rope"),
                     load(pool, head_gain_rows[:, :, :].rearrange("p a b -> p (a b)"),
                          dram["head_gain_rows"].partition_broadcast(P), "ld_head_gain_rows")]
        for st in stage_m:
            st.users = [table_out[-1], *spread_read]
        head_ss = [columns(4), columns(4)]
        scale128 = 128 ** -0.5
        dve.wait(ld["head_gain_cols"])
        q_gain = columns(4)
        q_gain_ready = ts(dve, q_gain, head_gain_cols[:, :], scale128, ALU.mult)
        gain_col = {"qa": q_gain[:, 0:1], "ka": head_gain_cols[:, 1:2], "qc": q_gain[:, 2:3],
                    "kc": head_gain_cols[:, 3:4], "qb": scale128, "kb": 1.0}
        dest = {"qa": qaT, "ka": kaT, "qb": qbT, "kb": kbT, "qc": qcT, "kc": kcT}
        head_ready = {k: [] for k in dest}

        def head_norms(stages, heads, staged):
            rotary = heads[0][0] in ("qb", "kb")
            runs, a = [], 0
            while a < 4:
                b = a
                while b < 4 and heads[b][0] == heads[a][0]:
                    b += 1
                runs.append((*heads[a], a, b))
                a = b

            def sums(t):
                for n in range(4):
                    s = square_sum(stages[t].view[:, n * P:(n + 1) * P], head_ss[t][:, n:n + 1], [staged[t]])
                return s

            def scale(t, root):
                v4 = stages[t].view[:, :].rearrange("p (a b) -> p a b", a=4)
                dve.wait(root)
                if not rotary:
                    return tt(dve, v4, v4, head_ss[t].unsqueeze(2).to_broadcast([P, 4, P]), ALU.mult)
                dve.wait(*tab_ready)
                for n in range(4):
                    g = head_gain_rows[:, 0 if heads[n][0] == "qb" else 1, :]
                    s = stt(v4[:, n, :], v4[:, n, :], head_ss[t][:, n:n + 1], g, ALU.mult, ALU.mult)
                return s

            def rotate(t, s):
                st = stages[t]
                pairs = st.view[:, :].rearrange("p (a d two) -> p a d two", a=4, two=2)
                outs = turned.view[:, :].rearrange("p (a d two) -> p a d two", a=4, two=2)
                cos = rope[:, 0, t, :].unsqueeze(1).to_broadcast([P, 4, 64])
                sin = rope[:, 1, t, :].unsqueeze(1).to_broadcast([P, 4, 64])
                x0, x1 = pairs[:, :, :, 0], pairs[:, :, :, 1]
                dve.wait(s, *turned.users)
                m1 = tt(dve, outs[:, :, :, 0], x0, cos, ALU.mult)
                m2 = tt(dve, rope_work[:, :, :], x1, sin, ALU.mult)
                dve.wait(m1, m2)
                m = tt(dve, outs[:, :, :, 0], outs[:, :, :, 0], rope_work[:, :, :], ALU.subtract)
                yield
                m1 = tt(dve, outs[:, :, :, 1], x0, sin, ALU.mult)
                dve.wait(m)
                m2 = tt(dve, rope_work[:, :, :], x1, cos, ALU.mult)
                dve.wait(m1, m2)
                s = tt(dve, outs[:, :, :, 1], outs[:, :, :, 1], rope_work[:, :, :], ALU.add)
                st.users = [s]
                yield
                return s

            def turn_heads(t, src, s):
                bank = take("misc", misc)
                pe.wait(s)
                done = turn_tiles(bank.view, [src.view[:, i * P:(i + 1) * P] for i in range(4)])
                src.users = [done]
                act.wait(done, q_gain_ready, ld["head_gain_cols"])
                for kind, first, a, b in runs:
                    c = scaled(dest[kind][:, first:first + b - a, t * P:(t + 1) * P],
                               bank.view[:, a * P:b * P].rearrange("p (a b) -> p a b", a=b - a), gain_col[kind])
                    head_ready[kind].append(c)
                bank.users = [c]

            s0 = sums(0)
            yield
            root0 = inverse_root(head_ss[0], head_ss[0], P, [s0])
            s1 = sums(1)
            yield
            root1 = inverse_root(head_ss[1], head_ss[1], P, [s1])
            s = scale(0, root0)
            yield
            if rotary:
                s = yield from rotate(0, s)
                turn_heads(0, turned, s)
                s = scale(1, root1)
                yield
                s = yield from rotate(1, s)
                turn_heads(1, turned, s)
            else:
                s1 = scale(1, root1)
                turn_heads(0, stages[0], s)
                yield
                turn_heads(1, stages[1], s1)

        stage_task = {}

        def project_heads(name, b, left, row_scale, ready, stages, heads):
            slot, done = stream_block(name, b, left)
            if stages[0] in stage_task:
                finish(stage_task[stages[0]])
            act.wait(*ready, done)
            staged = []
            for t in range(2):
                act.wait(*stages[t].users)
                staged.append(scaled(stages[t].view[:, :], slot.view[:, t, :], row_scale[:, t:t + 1]))
            slot.users = staged
            task = stage_task[stages[0]] = head_norms(stages, heads, staged)
            movers.append(task)
            return task

        def project_values(name, b, left, row_scale, ready, spans):
            slot, done = stream_block(name, b, left)
            act.wait(*ready, done)
            got = []
            for to, c0, b0, n in spans:
                for t in range(2):
                    got.append(scaled(to[:, t, c0:c0 + n], slot.view[:, t, b0:b0 + n], row_scale[:, t:t + 1]))
            slot.users = got
            return got

        kc_task = project_heads("w_mem", 0, mem_left, r_mem, mem_root, stage_m,
                                [("kc", i) for i in range(4)])
        got_vc = project_values("w_mem", 1, mem_left, r_mem, mem_root, [(vc, 0, 0, BW)])
        finish(norm_task)
        finish(kc_task)
        rr = r12_ready
        qc_task = project_heads("w_in2", 0, u2, r12, rr, stage, [("qc", i) for i in range(4)])

        prob2 = [Slot(spot(f"prob2_{i}", 40 + 2 * i, [2, SEQ])) for i in range(2)]
        prob2T = [Slot(spot(f"prob2T_{i}", 44 + 2 * i, [2, SEQ])) for i in range(2)]
        y_cross = Split("y_cross", 4, Q_AT + 36 * KB)
        y_gqa = Split("y_gqa", 6, Q_AT + 24 * KB)
        y_dil = Split("y_dil", 2, Q_AT + 44 * KB)
        stat2 = [columns(4), columns(4)]

        def dense_attention(n_heads, q, k, v, group, y, norms, ready):
            while norms in movers:
                yield
            for h in range(n_heads):
                kv = h // group
                p, pT = prob2[h % 2], prob2T[h % 2]
                nm, total = stat2[h % 2][:, 0:2], stat2[h % 2][:, 2:4]
                bank = take("misc", misc)
                pe.wait(*ready())
                for qt in range(2):
                    t = matmul_done(bank.view[:, qt * SEQ:(qt + 1) * SEQ], q[:, h, qt * P:(qt + 1) * P], k[:, kv, :],
                                    start=qt == 0)
                s = bank.view[:, :].rearrange("p (a b) -> p a b", a=2)
                dve.wait(t)
                t = dve.do(lambda e, nm=nm, s=s: e.tensor_reduce(nm, s, AX, ALU.max, negate=True))
                yield
                act.wait(t, *p.users)
                for qt in range(2):
                    t = activate(p.view[:, qt, :], s[:, qt, :], ACT.Exp, bias=nm[:, qt:qt + 1],
                                 accum_out=total[:, qt:qt + 1])
                bank.users = [t]
                yield
                dve.wait(t)
                t = dve.do(lambda e, total=total: e.reciprocal(total, total))
                yield
                act.wait(t)
                for qt in range(2):
                    t = scaled(p.view[:, qt, :], p.view[:, qt, :], total[:, qt:qt + 1])
                yield
                bank = take("misc", misc)
                pe.wait(t)
                done = turn_tiles(bank.view, [p.view[:, qt, st * P:(st + 1) * P] for st in range(2) for qt in range(2)])
                p.users = [done]
                yield
                act.wait(done, *pT.users)
                t = scaled(pT.view[:, :, :], bank.view[:, :].rearrange("p (a b) -> p a b", a=2), 1.0)
                bank.users = [t]
                yield
                bank = take("misc", misc)
                pe.wait(t)
                for st in range(2):
                    done = matmul_done(bank.view[:, 0:SEQ], v[:, st, kv * P:(kv + 1) * P], pT.view[:, st, :],
                                       st == 0, st == 1)
                pT.users = [done]
                yield
                bank.users = split_store([(y.hi[:, h, :], y.lo[:, h, :], bank.view[:, 0:SEQ], None)], [done])
                y.wrote([h], bank.users)
                yield

        cross_task = dense_attention(4, qcT, kcT, vc, 1, y_cross, qc_task,
                                     lambda: [*head_ready["qc"], *head_ready["kc"], *got_vc])
        tasks.append(cross_task)
        project_heads("w_in2", 1, u2, r12, rr, stage, [("qb", j) for j in range(4)])
        kb_task = project_heads("w_in2", 2, u2, r12, rr, stage, [("qb", 4), ("qb", 5), ("kb", 0), ("kb", 1)])
        got_vb = project_values("w_in2", 3, u2, r12, rr, [(vb, 0, 0, 2 * P), (va, 0, 2 * P, 2 * P)])
        gqa_task = dense_attention(6, qbT, kbT, vb, 3, y_gqa, kb_task,
                                   lambda: [*head_ready["qb"], *head_ready["kb"], *got_vb])
        tasks.append(gqa_task)
        got_va = got_vb + project_values("w_in2", 4, u2, r12, rr, [(va, 2 * P, 0, BW)])
        heads_a = [("qa", i) for i in range(6)] + [("ka", i) for i in range(6)]
        for g in range(3):
            a_task = project_heads("w_in2", 5 + g, u2, r12, rr, stage, heads_a[4 * g:4 * g + 4])
        probd = [Slot(spot(f"probd{i}", 28 + 3 * i, [3, SEQ])) for i in range(2)]
        probdT = [Slot(spot(f"probdT{i}", 34 + 3 * i, [3, 2, P])) for i in range(2)]
        skew_port = [Port(pool, f"bias_landed{i}") for i in range(2)]

        def dilated_attention():
            while a_task in movers:
                yield
            pool.wait(*y_cross.tickets(3))
            bias_in = {}

            def fetch(i):
                hh, qt = divmod(i, 2)
                p = probd[i % 2]
                pool.wait(*p.users, *table_out)
                for g in range(3):
                    rows = toeplitz[2 * g + hh]
                    skew = bass.AP(rows.tensor, rows.offset + 255 - P * qt, [[BW - 1, P], [1, SEQ]])
                    bias_in[i] = skew_port[i % 2].move(p.view[:, g, :], skew)

            fetch(0)
            yield
            for i in range(4):
                hh, qt = divmod(i, 2)
                p, pT = probd[i % 2], probdT[i % 2]
                if i < 3:
                    fetch(i + 1)
                nm, total = stat2[i % 2][:, 0:1], stat2[i % 2][:, 2:3]
                dve.wait(bias_in[i])
                for g in range(3):
                    bank = take("misc", misc)
                    pe.wait(*head_ready["qa"], *head_ready["ka"])
                    done = matmul_done(bank.view[:, 0:SEQ], qaT[:, 2 * g + hh, qt * P:(qt + 1) * P],
                                       kaT[:, 2 * g + hh, :])
                    dve.wait(done)
                    t = tt(dve, p.view[:, g, :], bank.view[:, 0:SEQ], p.view[:, g, :], ALU.add)
                    bank.users = [t]
                    yield
                flat = p.view[:, :, :].rearrange("p a b -> p (a b)")
                dve.wait(t)
                t = dve.do(lambda e, nm=nm, flat=flat: e.tensor_reduce(nm, flat, AX, ALU.max, negate=True))
                yield
                act.wait(t)
                t = activate(flat, flat, ACT.Exp, bias=nm, accum_out=total)
                yield
                dve.wait(t)
                t = dve.do(lambda e, total=total: e.reciprocal(total, total))
                dve.wait(t)
                t = ts(dve, flat, flat, total, ALU.mult)
                yield
                yield
                for half in range(2):
                    bank = take("misc", misc)
                    pe.wait(t)
                    done = turn_tiles(bank.view, [flat[:, (3 * half + n) * P:(3 * half + n + 1) * P] for n in range(3)])
                    act.wait(done, *pT.users)
                    c = scaled(pT.view[:, :, :, :].rearrange("p a b c -> p (a b c)")[:, 384 * half:384 * (half + 1)],
                               bank.view[:, 0:384], 1.0)
                    bank.users = [c]
                p.users = [done]
                yield
                bank = take("misc", misc)
                pe.wait(c, *got_va)
                for n in range(6):
                    g, st = divmod(n, 2)
                    done = matmul_done(bank.view[:, 0:P], va[:, st, (2 * g + hh) * P:(2 * g + hh + 1) * P],
                                       pT.view[:, g, st, :], n == 0, n == 5)
                pT.users = [done]
                yield
                o = slice(qt * P, (qt + 1) * P)
                bank.users = split_store([(y_dil.hi[:, hh, o], y_dil.lo[:, hh, o], bank.view[:, 0:P], None)], [done])
                y_dil.wrote([hh], bank.users, parts=2)
                yield

        dil_task = dilated_attention()
        tasks.append(dil_task)

        class ScaledGates:

            def before(self, n, c, gate):
                return None

            def evacuate(self, slot, done, gate, _):
                finish(a_task)
                act.wait(done, *gate.users, half_r12_ready, *[u for s in (*stage, turned) for u in s.users])
                for t in range(2):
                    g = activate(gate.view[:, t, :], slot.view[:, t, :], ACT.Tanh, scale=half_r12[:, t:t + 1])
                slot.users = [g]
                return [g]

        half_r12 = columns(2)
        dve.wait(*r12_ready)
        half_r12_ready = ts(dve, half_r12, r12, 0.5, ALU.mult)
        for g in gate_slots:
            g.users = []
        merged2 = Split("m2", KT, R_AT)
        mix("2", u2, [(y_cross, 4, cross_task), (y_gqa, 6, gqa_task), (y_dil, 2, dil_task)],
            mixed, gate_slots, ScaledGates(), mixed_to_left(merged2))

        v2 = Split("v2", KT, U_AT)
        squares3 = columns(8)
        ready = residual_blocks("w_out2", merged2, 0.5, squares3, v2, gains[:, 4, :])
        for s in silu:
            s.users = []
        half_r, half_r2, r_ready = ffn_rows(squares3, ready)
        stored = []

        def store(j, t, m):
            sp.wait(m)
            cs = slice(j * BW, (j + 1) * BW)
            stored.append(load(sp, out[t, :, cs], resid[:, t, cs], f"stored{j}_{t}"))

        ffn(("w_ffn_gate2", "w_ffn_up2", "w_ffn_down2"), v2, half_r, half_r2, r_ready, None, None, None, store)
        while movers or tasks:
            step_background()
        assert stream["half"] == len(halves)
        sp.wait(*stored)

        block = ctx.enter_context(nc.Block())
        block.sync(sp.emit)
        block.gpsimd(pool.emit)
        block.scalar(act.emit)
        block.vector(dve.emit)
        block.tensor(pe.emit)


def blocks(w, width=BW):
    k, n = w.shape
    return np.ascontiguousarray(w.reshape(k // P, P, n // width, width).transpose(2, 1, 0, 3)
                                .reshape(n // width, P, (k // P) * width))


def column(v):
    return np.ascontiguousarray(v.reshape(-1, P).T)


def constants():
    pos = np.arange(P, dtype=np.float32)
    diff = pos[:, None] - pos[None, :]
    far = np.float32(1e32)
    diag = np.where(diff >= 0, diff, far).astype(np.float32)
    off = diff + P
    band = np.where(off < 128, off, far).astype(np.float32)
    n = np.abs(np.arange(-255, 257))
    rel = np.arange(-255, 257)
    nb, exact = 16, 8
    large = exact + (np.log(np.maximum(n, 1).astype(np.float32) / exact)
                     / math.log(1024 / exact) * (nb - exact)).astype(np.int32)
    bucket = np.where(rel > 0, nb, 0) + np.where(n < exact, n, np.minimum(large, nb - 1))
    onehots = np.zeros((3, 33, 512), np.float32)
    for g, dil in enumerate((1, 4, 16)):
        valid = (rel % dil == 0) & (n // dil <= 64)
        for i in np.nonzero(valid)[0]:
            onehots[g, bucket[i], i] = 1.0
        onehots[g, 32] = np.where(valid, 0.0, MASKED)
    inv = 10000.0 ** (-np.arange(32, dtype=np.float32) / 32)
    tok = np.arange(SEQ)
    ang = np.concatenate([(tok // 64).astype(np.float32)[:, None] * inv,
                          (tok % 64).astype(np.float32)[:, None] * inv], axis=-1).astype(np.float32)
    rope = np.stack([np.cos(ang), np.sin(ang)]).astype(np.float32).reshape(2, 2, P, 64).transpose(2, 0, 1, 3)
    fox_select = np.zeros((36, 10), np.float32)
    fox_select[:4, :4], fox_select[32:, 4:8] = np.eye(4), -np.eye(4)
    fox_select[32:, 8] = fox_select[:4, 9] = 1.0
    return {
        "c_ident": np.eye(P, dtype=np.float32),
        "c_diag_mask": np.where(diff >= 0, 0.0, MASKED).astype(np.float32),
        "c_dist_a": np.concatenate([diag, off, diag], 1).astype(np.float32),
        "c_dist_d": np.concatenate([diag, band, diag], 1).astype(np.float32),
        "c_fox_select": fox_select,
        "c_onehots": onehots,
        "c_rope": np.ascontiguousarray(rope),
    }


def lay_out(i):
    w = i["w_in"][0]
    at = np.cumsum((0, 512, 512, 512, 512, 512, 512, 512, 512, 4, 512, 128, 128, 8192))
    aq, ak, av, bx, bg, cq, ck, cv, cf, dq, dk, dv, gz = (w[:, a:b] for a, b in zip(at[:-1], at[1:]))
    pair = np.concatenate([np.r_[64 * j:64 * j + 64, 256 + 64 * j:256 + 64 * j + 64] for j in range(4)])
    a = {}
    a["w_in"] = blocks(np.concatenate([bx, bg, aq, ak, av, dq[:, pair], cq, ck, cv], 1))
    a["w_in_misc"] = blocks(np.concatenate([dk, cf, dv], 1), P + 4 + P)
    order = (1, 0, 3, 2)
    a["w_gates"] = blocks(np.concatenate([gz[:, n * D:(n + 1) * D] for n in order], 1))
    a["b_gate"] = np.concatenate([i["b_gate"][:, n * D:(n + 1) * D] for n in order], 1)
    for k, n in enumerate(order):
        wb = i["w_branch"][0, n]
        a[f"w_branch{k}"] = blocks(wb[pair] if n == 3 else wb)
    a["w_out"] = blocks(i["w_out"][0])
    a["w_ffn_gate"], a["w_ffn_up"] = blocks(i["w_ffn_gate"][0]), blocks(i["w_ffn_up"][0])
    a["w_ffn_down"] = blocks(i["w_ffn_down"][0])
    a["x"] = i["x"].reshape(2, P, D)
    a["mem"] = i["mem_2"].reshape(2, P, D)
    a["gains"] = np.stack([column(i[n].reshape(-1)) for n in
                           ("norm_mix", "norm_ffn", "norm_final", "g_mix_2", "g_ffn_2", "g_mem_2")], 1)
    a["norm_final"] = i["norm_final"].reshape(1, D)
    a["lru_cols"] = np.stack([column(i["lru_conv_w"][0, j]) for j in range(4)] +
                             [column(i[n][0]) for n in ("lru_conv_b", "lru_ba", "lru_bx", "lru_lambda")], 1)
    diag = np.zeros((2, 4, P, P), np.float32)
    for g, n in enumerate(("lru_wa", "lru_wx")):
        for b in range(8):
            s = slice(64 * (b % 2), 64 * (b % 2) + 64)
            diag[g, b // 2, s, s] = i[n][0, b]
    a["lru_gate_w"] = diag.reshape(8, P, P).transpose(1, 0, 2)
    a["lam_vectors"] = np.concatenate([i[n] for n in ("diff_lq1", "diff_lk1", "diff_lq2", "diff_lk2")], 1)
    a["subln_col"] = i["diff_subln"].reshape(P, 1)
    a["fox_bias"] = np.concatenate([i["fox_b_f"], np.zeros((1, 28), np.float32), i["fox_b_f"]], 1).reshape(36, 1)
    a["sinks"] = i["swa_sinks"].reshape(1, 8)
    w = i["w_in_2"][0]
    at = np.cumsum((0, 768, 768, 768, 768, 256, 256, 512, 6144))
    qa, ka, va, qb, kb, vb, qc, gz = (w[:, x:y] for x, y in zip(at[:-1], at[1:]))
    a["w_in2"] = blocks(np.concatenate([qc, qb, kb, vb, va, qa, ka], 1))
    order = (2, 1, 0)
    a["w_gates2"] = blocks(np.concatenate([gz[:, n * D:(n + 1) * D] for n in order], 1))
    for k, n in enumerate(("w_br_c_2", "w_br_b_2", "w_br_a_2")):
        a[f"w_branch2{k}"] = blocks(i[n][0])
    a["w_mem"] = blocks(i["w_mem_kv_2"][0])
    a["w_out2"] = blocks(i["w_o_2"][0])
    a["w_ffn_gate2"] = blocks(i["w_ffn_in_2"][0][:, :D_FF])
    a["w_ffn_up2"] = blocks(i["w_ffn_in_2"][0][:, D_FF:])
    a["w_ffn_down2"] = blocks(i["w_ffn_out_2"][0])
    a["head_gain_cols"] = np.stack([i[n].reshape(P) for n in ("g_qa_2", "g_ka_2", "g_qc_2", "g_kc_2")], 1)
    a["head_gain_rows"] = np.concatenate([i["g_qb_2"], i["g_kb_2"]], 1)
    a["table"] = i["rel_bias_2"]
    a.update(constants())
    return {n: np.ascontiguousarray(v) for n, v in a.items()}


def kernel(**inputs):
    import concourse.bacc as bacc
    from concourse.bass_utils import run_bass_kernel_spmd

    arrays = lay_out({n: np.asarray(v) for n, v in inputs.items()})
    nc = bacc.Bacc("TRN2", target_bir_lowering=False, num_devices=1)
    dram = {n: nc.dram_tensor(f"in_{n}", v.shape, mybir.dt.from_np(v.dtype), kind="ExternalInput").ap()
            for n, v in arrays.items()}
    dram["scratch_bias"] = nc.dram_tensor("scratch_bias", (6, P, BW), F32, kind="Internal").ap()
    out = nc.dram_tensor("out_tokens", (2, P, D), F32, kind="ExternalOutput").ap()
    build(nc, dram, out)
    got = run_bass_kernel_spmd(nc, [{f"in_{n}": v for n, v in arrays.items()}], core_ids=[0])
    return got.results[0]["out_tokens"].reshape(1, SEQ, D)
```
